# Optimizing a Trainium2 kernel written in Bass

```python
import math
import jax
import jax.numpy as jnp
from jax import lax
import numpy as np

D_MODEL = 1024
BATCH = 1
SEQ = 512
DEPTH = 1

EPS = 1e-5
GLA_HEADS = 4
GLA_DK = 128
GLA_DV = 256
GLA_RANK = 16
GLA_TAU = 16.0
GLA_CHUNK = 64
GLA_QK_DIM = GLA_HEADS * GLA_DK
GLA_V_DIM = GLA_HEADS * GLA_DV
SSD_DINNER = 2 * D_MODEL
SSD_HEADDIM = 64
SSD_HEADS = SSD_DINNER // SSD_HEADDIM
SSD_GROUPS = 4
SSD_HPG = SSD_HEADS // SSD_GROUPS
SSD_STATE = 128
SSD_CONV = 4
SSD_CONV_PAD = (1, 2)
SSD_CHUNK = 64
SSD_BC_DIM = SSD_GROUPS * SSD_STATE
SSD_CONV_DIM = SSD_DINNER + 2 * SSD_BC_DIM
N_EXPERTS = 32
TOP_K = 4
D_FF = D_MODEL
SWIGLU_LIMIT = 7.0
SWIGLU_ALPHA = 1.702
MOE_BLOCK = 128
IN_WIDTHS = (GLA_QK_DIM, GLA_QK_DIM, GLA_V_DIM, GLA_V_DIM, GLA_RANK, GLA_RANK,
             SSD_DINNER, SSD_CONV_DIM, 2 * SSD_HEADS, D_MODEL, D_MODEL)
D_IN_PROJ = sum(IN_WIDTHS)

kernel_name = 'hybrid_gla_ssd_moe_block'

def _split_points():
    pts, acc = [], 0
    for w in IN_WIDTHS[:-1]:
        acc += w
        pts.append(acc)
    return pts

def rmsnorm(t, g):
    t32 = t.astype(jnp.float32)
    t32 = t32 * lax.rsqrt(jnp.mean(t32 * t32, axis=-1, keepdims=True) + EPS)
    return t32.astype(t.dtype) * g

def _flip(t):
    return jnp.flip(t, axis=1)

def _chunks(t, c):
    b, s = t.shape[:2]
    return jnp.moveaxis(t.reshape((b, s // c, c) + t.shape[2:]), 1, 0)

def _unchunks(t):
    t = jnp.moveaxis(t, 0, 1)
    return t.reshape((t.shape[0], t.shape[1] * t.shape[2]) + t.shape[3:])

def gla_scan(q, k, v, log_a):
    c = GLA_CHUNK
    mask = jnp.tril(jnp.ones((c, c), dtype=bool))

    def step(state, inp):
        qc, kc, vc, gc = inp
        b = jnp.cumsum(gc, axis=1)
        b_mid = b[:, c // 2][:, None]
        qs = qc * jnp.exp(b - b_mid)
        ks = kc * jnp.exp(b_mid - b)
        s = jnp.where(mask, jnp.einsum('bihk,bjhk->bhij', qs, ks), 0.0)
        o = jnp.einsum('bhij,bjhv->bihv', s, vc)
        o = o + jnp.einsum('bihk,bhkv->bihv', qc * jnp.exp(b), state)
        b_last = b[:, -1]
        kd = kc * jnp.exp(b_last[:, None] - b)
        state = state * jnp.exp(b_last)[..., None] + jnp.einsum('bjhk,bjhv->bhkv', kd, vc)
        return state, o

    state0 = jnp.zeros((q.shape[0], GLA_HEADS, GLA_DK, GLA_DV), jnp.float32)
    _, o = lax.scan(step, state0, (_chunks(q, c), _chunks(k, c), _chunks(v, c), _chunks(log_a, c)))
    return _unchunks(o)

def ssd_scan(x, dt, a, bm, cm):
    c = SSD_CHUNK
    mask = jnp.tril(jnp.ones((c, c), dtype=bool))[:, :, None, None]

    def step(state, inp):
        xc, dtc, bc, cc = inp
        cum = jnp.cumsum(dtc * a, axis=1)
        seg = cum[:, :, None] - cum[:, None, :]
        decay = jnp.exp(jnp.where(mask, seg, -jnp.inf))
        cb = jnp.einsum('bign,bjgn->bijg', cc, bc)
        w = cb[..., None] * decay * dtc[:, None]
        y = jnp.einsum('bijgr,bjgrp->bigrp', w, xc)
        y = y + jnp.einsum('bign,bgrpn->bigrp', cc, state) * jnp.exp(cum)[..., None]
        to_end = jnp.exp(cum[:, -1:] - cum) * dtc
        state = state * jnp.exp(cum[:, -1])[..., None, None] + jnp.einsum('bjgn,bjgr,bjgrp->bgrpn', bc, to_end, xc)
        return state, y

    state0 = jnp.zeros((x.shape[0], SSD_GROUPS, SSD_HPG, SSD_HEADDIM, SSD_STATE), jnp.float32)
    _, y = lax.scan(step, state0, (_chunks(x, c), _chunks(dt, c), _chunks(bm, c), _chunks(cm, c)))
    return _unchunks(y)

def dwconv(t, w, b):
    y = lax.conv_general_dilated(t, w[:, None, :], window_strides=(1,), padding=[SSD_CONV_PAD],
                                 dimension_numbers=('NWC', 'WIO', 'NWC'), feature_group_count=t.shape[-1])
    return y + b

def moe(xn, w_router, b_router, w1, b1, w2, b2):
    bsz, s, d = xn.shape
    t = bsz * s
    n_assign = t * TOP_K
    xt = xn.reshape(t, d)
    logits = (xt @ w_router + b_router).astype(jnp.float32)
    top_v, top_i = lax.top_k(logits, TOP_K)
    gates = jax.nn.softmax(top_v, axis=-1)
    flat_e = top_i.reshape(-1)
    flat_tok = jnp.arange(n_assign, dtype=jnp.int32) // TOP_K
    flat_g = gates.reshape(-1)
    order = jnp.argsort(flat_e)
    e_sorted = flat_e[order]
    counts = jnp.bincount(flat_e, length=N_EXPERTS)
    padded = (counts + MOE_BLOCK - 1) // MOE_BLOCK * MOE_BLOCK
    start = jnp.cumsum(counts) - counts
    pend = jnp.cumsum(padded)
    pstart = pend - padded
    rank = jnp.arange(n_assign, dtype=jnp.int32) - start[e_sorted]
    dest = pstart[e_sorted] + rank
    n_pad = n_assign + N_EXPERTS * MOE_BLOCK
    n_blocks = n_pad // MOE_BLOCK
    tok_buf = jnp.full((n_pad,), t, jnp.int32).at[dest].set(flat_tok[order])
    gate_buf = jnp.zeros((n_pad,), jnp.float32).at[dest].set(flat_g[order])
    blk_e = jnp.minimum(jnp.searchsorted(pend, jnp.arange(n_blocks, dtype=jnp.int32) * MOE_BLOCK, side='right'),
                        N_EXPERTS - 1)
    x_pad = jnp.concatenate([xt, jnp.zeros((1, d), xt.dtype)], axis=0)
    xb = x_pad[tok_buf].reshape(n_blocks, MOE_BLOCK, d)

    def expert_block(args):
        xblk, e = args
        hdn = xblk @ w1[e] + b1[e]
        gate = jnp.minimum(hdn[..., :D_FF], SWIGLU_LIMIT)
        lin = jnp.clip(hdn[..., D_FF:], -SWIGLU_LIMIT, SWIGLU_LIMIT)
        act = gate * jax.nn.sigmoid(SWIGLU_ALPHA * gate) * (lin + 1.0)
        return act @ w2[e] + b2[e]

    yb = lax.map(expert_block, (xb, blk_e)).reshape(n_pad, d)
    yb = yb * gate_buf[:, None].astype(yb.dtype)
    out = jnp.zeros((t + 1, d), yb.dtype).at[tok_buf].add(yb)[:t]
    return out.reshape(bsz, s, d)

def hybrid_layer(h, norm_mix_g, w_in, gla_fw2_f, gla_fb_f, gla_fw2_b, gla_fb_b, gla_norm_g, conv_w, conv_b,
                 dt_bias_f, dt_bias_b, a_log_f, a_log_b, ssd_d, ssd_norm_g, w_up_gla, w_up_ssd, w_out,
                 norm_ffn_g, w_router, b_router, w1, b1, w2, b2):
    f32 = jnp.float32
    bsz, s, _ = h.shape
    xn = rmsnorm(h, norm_mix_g)
    proj = xn @ w_in
    q, k, v, r, lr_f, lr_b, z, xbc, dt_raw, g_gla, g_ssd = jnp.split(proj, _split_points(), axis=-1)

    q = (q.reshape(bsz, s, GLA_HEADS, GLA_DK) * GLA_DK ** -0.5).astype(f32)
    k = k.reshape(bsz, s, GLA_HEADS, GLA_DK).astype(f32)
    v = v.reshape(bsz, s, GLA_HEADS, GLA_DV).astype(f32)
    log_a_f = (jax.nn.log_sigmoid((lr_f @ gla_fw2_f + gla_fb_f).astype(f32)) / GLA_TAU).reshape(bsz, s, GLA_HEADS, GLA_DK)
    log_a_b = (jax.nn.log_sigmoid((lr_b @ gla_fw2_b + gla_fb_b).astype(f32)) / GLA_TAU).reshape(bsz, s, GLA_HEADS, GLA_DK)
    o = gla_scan(q, k, v, log_a_f) + _flip(gla_scan(_flip(q), _flip(k), _flip(v), _flip(log_a_b)))
    o = rmsnorm(o, gla_norm_g).reshape(bsz, s, GLA_V_DIM).astype(h.dtype) * jax.nn.silu(r)

    xbc = jax.nn.silu(dwconv(xbc, conv_w, conv_b))
    xs, bm, cm = jnp.split(xbc, [SSD_DINNER, SSD_DINNER + SSD_BC_DIM], axis=-1)
    xs = xs.reshape(bsz, s, SSD_GROUPS, SSD_HPG, SSD_HEADDIM).astype(f32)
    bm = bm.reshape(bsz, s, SSD_GROUPS, SSD_STATE).astype(f32)
    cm = cm.reshape(bsz, s, SSD_GROUPS, SSD_STATE).astype(f32)
    dt_f = jax.nn.softplus((dt_raw[..., :SSD_HEADS] + dt_bias_f).astype(f32)).reshape(bsz, s, SSD_GROUPS, SSD_HPG)
    dt_b = jax.nn.softplus((dt_raw[..., SSD_HEADS:] + dt_bias_b).astype(f32)).reshape(bsz, s, SSD_GROUPS, SSD_HPG)
    a_f = -jnp.exp(a_log_f.astype(f32)).reshape(SSD_GROUPS, SSD_HPG)
    a_b = -jnp.exp(a_log_b.astype(f32)).reshape(SSD_GROUPS, SSD_HPG)
    y = (ssd_scan(xs, dt_f, a_f, bm, cm)
         + _flip(ssd_scan(_flip(xs), _flip(dt_b), a_b, _flip(bm), _flip(cm)))
         + ssd_d.astype(f32).reshape(SSD_GROUPS, SSD_HPG, 1) * xs)
    y = y.reshape(bsz, s, SSD_DINNER) * jax.nn.silu(z.astype(f32))
    y = rmsnorm(y.reshape(bsz, s, SSD_GROUPS, SSD_DINNER // SSD_GROUPS),
                ssd_norm_g.reshape(SSD_GROUPS, SSD_DINNER // SSD_GROUPS))
    y = y.reshape(bsz, s, SSD_DINNER).astype(h.dtype)

    mix = jax.nn.sigmoid(g_gla) * (o @ w_up_gla) + jax.nn.sigmoid(g_ssd) * (y @ w_up_ssd)
    h = h + mix @ w_out

    h = h + moe(rmsnorm(h, norm_ffn_g), w_router, b_router, w1, b1, w2, b2)
    return h

def setup_inputs(seed: int = 0) -> dict:
    key = jax.random.key(seed)
    ks = iter(jax.random.split(key, 32))
    nrm = lambda shape, scale: jax.random.normal(next(ks), shape, jnp.float32) * scale
    gain = lambda shape: 1.0 + nrm(shape, 0.02)
    L = DEPTH
    u = jax.random.uniform(next(ks), (2, L, SSD_HEADS), jnp.float32)
    dt0 = jnp.exp(u * (math.log(0.1) - math.log(0.001)) + math.log(0.001))
    dt_bias = dt0 + jnp.log(-jnp.expm1(-dt0))
    a_log = jnp.log(jax.random.uniform(next(ks), (2, L, SSD_HEADS), jnp.float32, 1.0, 16.0))
    return {
        'x': nrm((BATCH, SEQ, D_MODEL), 1.0),
        'norm_mix_g': gain((L, D_MODEL)),
        'w_in': nrm((L, D_MODEL, D_IN_PROJ), D_MODEL ** -0.5),
        'gla_fw2_f': nrm((L, GLA_RANK, GLA_QK_DIM), GLA_RANK ** -0.5),
        'gla_fb_f': nrm((L, GLA_QK_DIM), 0.1),
        'gla_fw2_b': nrm((L, GLA_RANK, GLA_QK_DIM), GLA_RANK ** -0.5),
        'gla_fb_b': nrm((L, GLA_QK_DIM), 0.1),
        'gla_norm_g': gain((L, GLA_DV)),
        'conv_w': nrm((L, SSD_CONV, SSD_CONV_DIM), SSD_CONV ** -0.5),
        'conv_b': nrm((L, SSD_CONV_DIM), 0.02),
        'dt_bias_f': dt_bias[0],
        'dt_bias_b': dt_bias[1],
        'a_log_f': a_log[0],
        'a_log_b': a_log[1],
        'ssd_d': 1.0 + nrm((L, SSD_HEADS), 0.1),
        'ssd_norm_g': gain((L, SSD_DINNER)),
        'w_up_gla': nrm((L, GLA_V_DIM, D_MODEL), GLA_V_DIM ** -0.5),
        'w_up_ssd': nrm((L, SSD_DINNER, D_MODEL), SSD_DINNER ** -0.5),
        'w_out': nrm((L, D_MODEL, D_MODEL), D_MODEL ** -0.5),
        'norm_ffn_g': gain((L, D_MODEL)),
        'w_router': nrm((L, D_MODEL, N_EXPERTS), D_MODEL ** -0.5),
        'b_router': nrm((L, N_EXPERTS), 0.01),
        'w1': nrm((L, N_EXPERTS, D_MODEL, 2 * D_FF), D_MODEL ** -0.5),
        'b1': nrm((L, N_EXPERTS, 2 * D_FF), 0.01),
        'w2': nrm((L, N_EXPERTS, D_FF, D_MODEL), D_FF ** -0.5),
        'b2': nrm((L, N_EXPERTS, D_MODEL), 0.01),
        'norm_final_g': gain((D_MODEL,)),
    }

def reference(x, norm_mix_g, w_in, gla_fw2_f, gla_fb_f, gla_fw2_b, gla_fb_b, gla_norm_g, conv_w, conv_b,
              dt_bias_f, dt_bias_b, a_log_f, a_log_b, ssd_d, ssd_norm_g, w_up_gla, w_up_ssd, w_out,
              norm_ffn_g, w_router, b_router, w1, b1, w2, b2, norm_final_g):
    h = x
    for l in range(DEPTH):
        h = hybrid_layer(h, norm_mix_g[l], w_in[l], gla_fw2_f[l], gla_fb_f[l], gla_fw2_b[l], gla_fb_b[l],
                         gla_norm_g[l], conv_w[l], conv_b[l], dt_bias_f[l], dt_bias_b[l], a_log_f[l], a_log_b[l],
                         ssd_d[l], ssd_norm_g[l], w_up_gla[l], w_up_ssd[l], w_out[l], norm_ffn_g[l],
                         w_router[l], b_router[l], w1[l], b1[l], w2[l], b2[l])
    return rmsnorm(h, norm_final_g)


_drawn_inputs = setup_inputs


def setup_inputs(seed=0):
    import zlib

    import numpy as np

    out = dict(_drawn_inputs(seed))
    spreads = {}
    factors = {'gla_norm_g': 2.956, 'b1': 8.0, 'b2': 8.0, 'norm_final_g': 2.845}
    for name, (base, spread) in spreads.items():
        noise = np.random.default_rng([zlib.crc32(name.encode()), seed]).standard_normal(out[name].shape)
        drawn = base * np.exp(spread * noise) if base else spread * noise
        out[name] = jnp.asarray(drawn.astype(out[name].dtype))
    for name, factor in factors.items():
        out[name] = (out[name] * factor).astype(out[name].dtype)
    return out
```

```python
import numpy as np
from contextlib import ExitStack

import concourse.bass as bass
from concourse import mybir

F32 = mybir.dt.float32
I32 = mybir.dt.int32
F32R = mybir.dt.float32r
U32 = mybir.dt.uint32
ACT = mybir.ActivationFunctionType
ALU = mybir.AluOpType
AX = mybir.AxisListType

P = 128
SEQ = 512
D = 1024
NT = SEQ // P
NK = D // P
EPS = 1e-5

HEADS, DK, DV, RANK, TAU = 4, 128, 256, 16, 16.0
CH = 64
NCH = SEQ // CH
DIN, HD, SH, GR, NS = 2048, 64, 32, 4, 128
HPG = SH // GR
GW = DIN // GR
TAPS = 4
NCT = (DIN + 2 * GR * NS) // P
CQ, CK, CV, CR = 0, 512, 1024, 2048
CLF = 3072
CLB = CLF + RANK
CZ = CLB + RANK
CX = CZ + DIN
CB = CX + DIN
CC = CB + GR * NS
CDT = CC + GR * NS
CGG = CDT + 2 * SH
CGS = CGG + D
NE, TOPK, DFF = 32, 4, 1024
LIMIT, ALPHA = 7.0, 1.702
CAP = 96
ROUNDS = -(-SEQ // CAP)
SLOTS = ROUNDS * CAP
FAR = 4096.0

UNIT = 2048
SIDE = 8 * D + 2 * DFF // P * CAP
TEMPS = 25200 - SIDE
KG = P // CH

R_MIX, R_FFN, R_SSD, R_GLA, R_FBF, R_FBB = 0, 8, 16, 32, 34, 38
N_PAR = 42


def build(nc, x, norm_mix_g, w_in, fw2_f, fb_f, fw2_b, fb_b, gla_norm_g, conv_w, conv_b, dt_bias_f,
          dt_bias_b, a_log_f, a_log_b, ssd_d, ssd_norm_g, w_up_gla, w_up_ssd, w_out, norm_ffn_g,
          w_router, b_router, w1, b1, w2, b2, norm_final_g, out):
    with ExitStack() as ctx:
        def sem(name):
            return ctx.enter_context(nc.semaphore(name))

        def sb(name, cols, dt=F32):
            return ctx.enter_context(nc.sbuf_tensor(name, [P, cols], dt))

        ps = ctx.enter_context(nc.psum_tensor("ps", [P, 8, 512], F32))

        cum_d = nc.dram_tensor("cum_rows", (NT, GR, 2, HPG, P), F32).ap()
        y_d = nc.dram_tensor("ssd_out_T", (GR, P, GW // P * SEQ), F32).ap()
        xn_d = nc.dram_tensor("ffn_rows", (SEQ, D), F32).ap()
        res_d = nc.dram_tensor("expert_rows", (TOPK * SEQ, D), F32).ap()

        weights = sb("weights", 12 * UNIT)

        def slot(s, k):
            return weights[:, s * UNIT:(s + 1) * UNIT].rearrange("p (k n) -> p k n", k=k)

        xnT = weights[:, 8 * UNIT:10 * UNIT].rearrange("p (c t) -> p c t", c=NK)
        oT = weights[:, 10 * UNIT:12 * UNIT].rearrange("p (c t) -> p c t", c=NK)

        ident = sb("ident", P)
        low = sb("low", P)
        high = sb("high", P)
        below = sb("below", P)
        ones = sb("ones", P)
        par_rows = sb("par_rows", 2 * P)
        par = sb("par", N_PAR)
        conv_par = sb("conv_par", (TAPS + 1) * NCT)
        b1T = sb("b1T", NE * 16)
        consts = sb("consts", 3 * 64 + SH + NE)
        dtb_bc = consts[:, 0:64]
        neg_a = consts[:, 64:128]
        d_bc = consts[:, 128:160]
        br_bc = consts[:, 160:192]
        stat = sb("stat", 64)
        dt_all = sb("dt_all", 5 * NT * 64)
        T = sb("temps", TEMPS)
        before_experts = ExitStack()
        T_side = before_experts.enter_context(nc.sbuf_tensor("side_temps", [P, SIDE], F32))

        used = {}

        def take_anew(main=0):
            used.update(main=main, side=0)

        def take(cols):
            at = used["main"]
            used["main"] += cols
            assert used["main"] <= TEMPS, used
            return T[:, at:at + cols]

        def take_side(cols):
            at = used["side"]
            used["side"] += cols
            assert used["side"] <= SIDE, used
            return T_side[:, at:at + cols]

        take_anew()

        x_in = sem("x_in")
        par_in = sem("par_in")
        bc_in = sem("bc_in")
        small_in = sem("small_in")
        fw_in = sem("fw_in")
        head_w = [sem(f"head_w{i}") for i in range(3)]
        group_w = [sem(f"group_w{i}") for i in range(5)]
        zeroed = sem("zeroed")
        apart = sem("apart")
        masks = sem("masks")
        par_T = sem("par_T")
        par_ok = sem("par_ok")
        x_sq = sem("x_sq")
        x_ms = sem("x_ms")
        x_sc = sem("x_sc")
        xT_ps = sem("xT_ps")
        xT_a = sem("xT_a")
        xT_v = sem("xT_v")
        proj_ready = sem("proj_ready")
        proj_taken = sem("proj_taken")
        gate_ps = sem("gate_ps")
        gate_a = sem("gate_a")
        gate_z = sem("gate_z")
        gate_ls = sem("gate_ls")
        gate_la = sem("gate_la")
        dta_ok = sem("dta_ok")
        cum_ps = sem("cum_ps")
        cum_v = sem("cum_v")
        cumT_ok = sem("cumT_ok")
        scan_ok = sem("scan_ok")
        dt_a = sem("dt_a")
        dt_v = sem("dt_v")
        cumT_out = sem("cumT_out")

        def dts(i):
            return dt_all[:, i * NT * 64:(i + 1) * NT * 64].rearrange("p (t h) -> p t h", t=NT)

        dt_n, cum_n, ecum_n, dend_n, etot_n = (dts(i) for i in range(5))

        cumg = take(2 * HEADS * SEQ)
        lr_T = take(SEQ)
        fw2 = take(HEADS * DK)
        reset = take(SEQ)
        gmask = take(2 * NT * CH)
        scan_from = used["main"]
        xw = take_side(NT * D)
        xw3 = xw.rearrange("p (t d) -> p t d", t=NT)
        wS = take(NK * 112)
        wS3 = wS.rearrange("p (k n) -> p k n", k=NK)
        junk = take_side(D)
        lsA = take_side(2 * SEQ)
        lsB = take_side(2 * SEQ)
        lsC = take_side(2 * SEQ)
        z_, e_, u_, r_, l_, a_, tot_, s_ = (take(NT * 64).rearrange("p (t h) -> p t h", t=NT) for _ in range(8))
        cum_T = take(SEQ)

        mix_w = [sem(f"mix_w{i}") for i in range(5)]
        out_w = [sem(f"out_w{i}") for i in range(4)]
        exp_w = [sem(f"exp_w{i}") for i in range(12)]

        def load_mix(sp, i, s):
            if s < 2:
                src = w_in[:, bass.ds(i * 256 + (CGG, CGS)[s], 256)]
            elif s == 2:
                src = w_up_gla[:, bass.ds(i * 256, 256)]
            else:
                src = w_up_ssd[(s - 3) * D:(s - 2) * D, bass.ds(i * 256, 256)]
            sp.dma_start(slot(s, NK), src.rearrange("(k p) n -> p k n", p=P)).then_inc(mix_w[s], 16)

        def load_out(sp, n):
            sp.dma_start(slot((5, 6, 7, 0)[n], NK), w_out[:, n * 256:(n + 1) * 256].rearrange("(k p) n -> p k n", p=P)).then_inc(out_w[n], 16)

        def load_expert(sp, it, u):
            e = it % NE
            if u < 8:
                src = w1.rearrange("e k n -> (e k) n")[bass.ds(e * D + u * P, P), :]
                sp.dma_start(slot(u, 1)[:, 0, :], src).then_inc(exp_w[u], 16)
            else:
                src = w2.rearrange("e k n -> (e k) n")[bass.ds(e * DFF + (u - 8) * 2 * P, 2 * P), :]
                sp.dma_start(slot(u, 2), src.rearrange("(k p) n -> p k n", p=P)).then_inc(exp_w[u], 16)

        def alone(eng):
            eng.sem_inc(apart, 1)

        def load_head(sp, h):
            s0 = slot(0, NK)
            sp.dma_start(s0[:, :, 0:DK], w_in[:, bass.ds(h * DK + CQ, DK)].rearrange("(k p) n -> p k n", p=P)).then_inc(head_w[0], 16)
            sp.dma_start(s0[:, :, DK:2 * DK], w_in[:, bass.ds(h * DK + CK, DK)].rearrange("(k p) n -> p k n", p=P)).then_inc(head_w[0], 16)

        def load_head_v(sp, h):
            sp.dma_start(slot(1, NK), w_in[:, bass.ds(h * DV + CV, DV)].rearrange("(k p) n -> p k n", p=P)).then_inc(head_w[1], 16)

        def load_head_r(sp, h):
            sp.dma_start(slot(2, NK), w_in[:, bass.ds(h * DV + CR, DV)].rearrange("(k p) n -> p k n", p=P)).then_inc(head_w[2], 16)

        def load_group_x(sp, g, half):
            sp.dma_start(slot(3 + half, NK), w_in[:, bass.ds(g * GW + CX + half * 256, 256)].rearrange("(k p) n -> p k n", p=P)).then_inc(group_w[half], 16)

        def load_group_bc(sp, g):
            s5 = slot(5, NK)
            sp.dma_start(s5[:, :, 0:NS], w_in[:, bass.ds(g * NS + CB, NS)].rearrange("(k p) n -> p k n", p=P)).then_inc(group_w[2], 16)
            sp.dma_start(s5[:, :, NS:2 * NS], w_in[:, bass.ds(g * NS + CC, NS)].rearrange("(k p) n -> p k n", p=P)).then_inc(group_w[2], 16)

        def load_group_z(sp, g, half):
            sp.dma_start(slot(6 + half, NK), w_in[:, bass.ds(g * GW + CZ + half * 256, 256)].rearrange("(k p) n -> p k n", p=P)).then_inc(group_w[3 + half], 16)

        hp_ready = sem("hp_ready")
        hp_taken = sem("hp_taken")
        v_kept = sem("v_kept")
        r_kept = sem("r_kept")
        g_diff = sem("g_diff")
        g_exp = sem("g_exp")
        g_dec = sem("g_dec")
        g_qk = sem("g_qk")
        s_ps = sem("s_ps")
        s_sel = sem("s_sel")
        kd_ps = sem("kd_ps")
        kd_ok = sem("kd_ok")
        st_ps = sem("st_ps")
        st_ok = sem("st_ok")
        o_ps = sem("o_ps")
        o_sq = sem("o_sq")
        o_v = sem("o_v")
        oT_ps = sem("oT_ps")
        oT_ok = sem("oT_ok")
        pads = sem("pads")

        take_anew(scan_from)
        r_raw, r_w = (take_side(2 * SEQ).rearrange("p (j t) -> p j t", j=2) for _ in range(2))
        g_e = [[take_side(SEQ) for _ in range(4)] for _ in range(2)]
        kd_n = take_side(2 * SEQ).rearrange("p (d t n) -> p d t n", d=2, t=NT)
        s_m = take_side(SEQ)
        v_w, v_raw = (take_side(NT * DV).rearrange("p (t n) -> p t n", t=NT) for _ in range(2))
        g_d = [[take(SEQ) for _ in range(2)] for _ in range(2)]
        s_w = take(SEQ // 2)
        o_n = take(NT * DV).rearrange("p (t n) -> p t n", t=NT)
        o_junk = take(DV)
        q_raw, k_raw = take(SEQ), take(SEQ)
        g_st = [take(DV) for _ in range(2)]
        dec = take(2 * NCH).rearrange("p (d c) -> p d c", d=2)
        LAST, MID = (CH - 1, 0), (CH // 2, CH // 2 - 1)

        def by_chunk(ap):
            return ap.rearrange("p (c i) -> p c i", i=CH)

        def head_piece(pe, h, n):
            if not (isinstance(h, int) and 8 * h + n < 2):
                pe.wait_ge(hp_taken, h * 8 + n - 1)
            if n in (0, 2, 6):
                pe.wait_ge(head_w[(0, 2, 6).index(n)], (h + 1) * (32 if n == 0 else 16))
            b = n % 2
            for k in range(NK):
                flags = dict(start=k == 0, stop=k == NK - 1)
                if n < 2:
                    last = nc.tensor.matmul(ps[:, b, :], slot(0, NK)[:, k, n * DK:(n + 1) * DK], xnT[:, k, :], **flags)
                elif n < 6:
                    t = n - 2
                    last = nc.tensor.matmul(ps[:, b, 0:DV], xnT[:, k, t * P:(t + 1) * P], slot(1, NK)[:, k, :], **flags)
                else:
                    j = n - 6
                    last = nc.tensor.matmul(ps[:, b, :], slot(2, NK)[:, k, j * P:(j + 1) * P], xnT[:, k, :], **flags)
            last.then_inc(hp_ready, 1)

        def head_take(act, h, n):
            act.wait_ge(hp_ready, h * 8 + n + 1)
            first = isinstance(h, int) and h == 0
            b = n % 2
            if n < 2:
                if n == 0 and not first:
                    act.wait_ge(g_qk, h * 8)
                nc.scalar.activation((q_raw, k_raw)[n], ps[:, b, :], ACT.Copy, scale=(DK ** -0.5, 1.0)[n]).then_inc(hp_taken, 1)
            elif n < 6:
                if n == 2 and not first:
                    act.wait_ge(v_kept, h)
                nc.scalar.activation(v_raw[:, n - 2, :], ps[:, b, 0:DV], ACT.Copy).then_inc(hp_taken, 1)
            else:
                if n == 6 and not first:
                    act.wait_ge(r_kept, h)
                nc.scalar.activation(r_raw[:, n - 6, :], ps[:, b, :], ACT.Silu).then_inc(hp_taken, 1)

        with nc.Block() as block:
            @block.sync
            def _(sp):
                for t in range(NT):
                    sp.dma_start(xw3[:, t, :], x[t * P:(t + 1) * P, :]).then_inc(x_in, 16)
                pr = par_rows
                for row, src, n in ((R_MIX, norm_mix_g, 8), (R_FFN, norm_ffn_g, 8), (R_SSD, ssd_norm_g, 16),
                                    (R_GLA, gla_norm_g, 2), (R_FBF, fb_f, 4), (R_FBB, fb_b, 4)):
                    sp.dma_start(pr[row:row + n, 0:P], src.rearrange("(n c) -> n c", c=P)).then_inc(par_in, 16)
                sp.dma_start(pr[0:TAPS * NCT, P:2 * P], conv_w.rearrange("k (n c) -> (k n) c", c=P)).then_inc(par_in, 16)
                sp.dma_start(pr[TAPS * NCT:(TAPS + 1) * NCT, P:2 * P], conv_b.rearrange("(n c) -> n c", c=P)).then_inc(par_in, 16)
                for c0, n, dst in ((CLF, RANK, 0), (CLB, RANK, 32), (CDT, 64, 48)):
                    sp.dma_start(wS3[:, :, dst:dst + n], w_in[:, c0:c0 + n].rearrange("(k p) n -> p k n", p=P)).then_inc(small_in, 16)
                load_head(sp, 0)
                load_head_v(sp, 0)
                load_head_r(sp, 0)
                for dst, src in ((dtb_bc[:, 0:SH], dt_bias_f), (dtb_bc[:, SH:64], dt_bias_b), (neg_a[:, 0:SH], a_log_f),
                                 (neg_a[:, SH:64], a_log_b), (d_bc, ssd_d), (br_bc, b_router)):
                    sp.dma_start(dst, src.rearrange("(a n) -> a n", a=1).broadcast_to([P, src.shape[0]])).then_inc(bc_in, 16)
                sp.dma_start(fw2[0:RANK, :], fw2_f).then_inc(fw_in, 16)
                sp.dma_start(fw2[32:32 + RANK, :], fw2_b).then_inc(fw_in, 16)
                load_group_x(sp, 0, 0)
                load_group_x(sp, 0, 1)
                load_group_bc(sp, 0)
                load_group_z(sp, 0, 0)
                load_group_z(sp, 0, 1)
                sp.wait_ge(cumT_ok, 1)
                for d in range(2):
                    for g in range(GR):
                        r0 = d * SH + g * HPG
                        sp.dma_start(cum_d[:, g, d, :, :].rearrange("t h i -> h t i"),
                                     cum_T[r0:r0 + HPG, :].rearrange("h (t i) -> h t i", t=NT)).then_inc(cumT_out, 16)
                sp.wait_ge(cumT_out, 16 * 8)

            @block.gpsimd
            def _(pool):
                nc.gpsimd.memset(ones[:], 1.0).then_inc(zeroed, 1)
                nc.gpsimd.memset(ident[:], 0.0).then_inc(zeroed, 1)
                nc.gpsimd.memset(reset, 1.0).then_inc(zeroed, 1)
                nc.gpsimd.memset(wS3[:, :, RANK:32], 0.0).then_inc(zeroed, 1)
                pool.wait_ge(zeroed, 4)
                nc.gpsimd.affine_select(out=ident[:], in_=ident[:], compare_op=ALU.not_equal, fill=1.0, base=0,
                                        pattern=[[-1, P]], channel_multiplier=1).then_inc(masks, 1)
                nc.gpsimd.affine_select(out=low[:], in_=ones[:], compare_op=ALU.is_ge, fill=0.0, base=0,
                                        pattern=[[1, P]], channel_multiplier=-1).then_inc(masks, 1)
                nc.gpsimd.affine_select(out=high[:], in_=ones[:], compare_op=ALU.is_ge, fill=0.0, base=0,
                                        pattern=[[-1, P]], channel_multiplier=1).then_inc(masks, 1)
                nc.gpsimd.affine_select(out=below[:], in_=ones[:], compare_op=ALU.is_ge, fill=0.0, base=-1,
                                        pattern=[[1, P]], channel_multiplier=-1).then_inc(masks, 1)
                nc.gpsimd.memset(reset.rearrange("p (c i) -> p c i", i=CH)[:, :, 0:1], 0.0).then_inc(masks, 1)

            @block.scalar
            def _(act):
                for t in range(NT):
                    act.wait_ge(x_in, 16 * NT)
                    if t:
                        act.wait_ge(x_sq, t)
                    nc.scalar.activation(junk, xw3[:, t, :], ACT.Square, accum_out=stat[:, t:t + 1]).then_inc(x_sq, 1)
                act.wait_ge(x_ms, 1)
                nc.scalar.activation(stat[:, 8:8 + NT], stat[:, 4:4 + NT], ACT.Sqrt).then_inc(x_sq, 1)
                for c in range(0, NK, 2):
                    act.wait_ge(xT_ps, c + 1)
                    act.wait_ge(par_ok, 2)
                    nc.scalar.activation(xnT[:, c, :], ps[:, 2, :], ACT.Copy, scale=par[:, R_MIX + c:R_MIX + c + 1]).then_inc(xT_a, 1)
                act.wait_ge(proj_ready, 1)
                nc.scalar.activation(lr_T[0:48, :], ps[0:48, 0, :], ACT.Copy).then_inc(proj_taken, 1)
                for h in range(HEADS):
                    act.wait_ge(gate_z, 2 * (h + 1))
                    if h:
                        act.wait_ge(gate_ls, h)
                    nc.scalar.activation(lsB, lsA, ACT.Abs).then_inc(gate_a, 1)
                    act.wait_ge(gate_a, 3 * h + 1)
                    nc.scalar.activation(lsB, lsB, ACT.Exp, scale=-1.0).then_inc(gate_a, 1)
                    act.wait_ge(gate_a, 3 * h + 2)
                    nc.scalar.activation(lsC, lsB, ACT.Ln, bias=1.0).then_inc(gate_a, 1)
                    for n in range(2 * h - 2, 2 * h):
                        if n >= 0:
                            head_take(act, 0, n)
                act.wait_ge(bc_in, 16 * 6)
                nc.scalar.activation(neg_a, neg_a, ACT.Exp).then_inc(dt_a, 1)
                act.wait_ge(dt_v, 2)
                nc.scalar.activation(e_, e_, ACT.Exp, scale=-1.0).then_inc(dt_a, 1)
                act.wait_ge(dt_v, 3)
                nc.scalar.activation(l_, u_, ACT.Ln).then_inc(dt_a, 1)
                act.wait_ge(cum_v, 3)
                nc.scalar.activation(ecum_n, cum_n, ACT.Exp).then_inc(dt_a, 1)
                nc.scalar.activation(dend_n, s_, ACT.Exp).then_inc(dt_a, 1)
                nc.scalar.activation(etot_n, tot_, ACT.Exp).then_inc(dt_a, 1)

            @block.vector
            def _(v):
                v.wait_ge(par_T, 1)
                nc.vector.tensor_copy(par[:, :], ps[:, 4, 0:N_PAR]).then_inc(par_ok, 1)
                v.wait_ge(par_T, 2)
                nc.vector.tensor_copy(conv_par[:, :], ps[:, 5, 0:(TAPS + 1) * NCT]).then_inc(par_ok, 1)
                v.wait_ge(x_sq, NT)
                nc.vector.tensor_scalar(stat[:, 4:4 + NT], stat[:, 0:NT], 1.0 / D, EPS, ALU.mult, ALU.add).then_inc(x_ms, 1)
                v.wait_ge(x_sq, NT + 1)
                nc.vector.reciprocal(stat[:, 12:12 + NT], stat[:, 8:8 + NT]).then_inc(x_ms, 1)
                v.wait_ge(x_ms, 2)
                for t in range(NT):
                    nc.vector.tensor_scalar(xw3[:, t, :], xw3[:, t, :], stat[:, 12 + t:13 + t], None, ALU.mult).then_inc(x_sc, 1)
                for c in range(1, NK, 2):
                    v.wait_ge(xT_ps, c + 1)
                    nc.vector.tensor_scalar(xnT[:, c, :], ps[:, 3, :], par[:, R_MIX + c:R_MIX + c + 1], None, ALU.mult).then_inc(xT_v, 1)
                v.wait_ge(masks, 5)
                for half in range(KG):
                    q = slice(half * CH, (half + 1) * CH)
                    for d, m in ((0, low), (1, high)):
                        nc.vector.tensor_copy(gmask[q, :].rearrange("p (d t i) -> p d t i", d=2, t=NT)[:, d],
                                              m[q, q].unsqueeze(1).broadcast_to([CH, NT, CH])).then_inc(scan_ok, 1)
                v.wait_ge(proj_ready, 2)
                v.wait_ge(bc_in, 16 * 6)
                raw = ps[:, 1, 0:256].rearrange("p (t h) -> p t h", t=NT)
                nc.vector.tensor_tensor(z_, raw, dtb_bc.unsqueeze(1).broadcast_to([P, NT, 64]), ALU.add).then_inc(dt_v, 1)
                v.wait_ge(dt_v, 1)
                nc.vector.scalar_tensor_tensor(e_, z_, -1.0, z_, ALU.mult, ALU.max).then_inc(dt_v, 1)
                for h in range(HEADS):
                    v.wait_ge(gate_ps, h + 1)
                    if h:
                        v.wait_ge(scan_ok, 4 + 2 * h)
                    for d in range(2):
                        nc.vector.tensor_scalar(lsA[:, d * SEQ:(d + 1) * SEQ], ps[:, 4 + 2 * (h % 2) + d, :],
                                                par[:, R_FBF + 4 * d + h:R_FBF + 4 * d + h + 1], None, ALU.add).then_inc(gate_z, 1)
                    v.wait_ge(gate_z, 2 * (h + 1))
                    v.wait_ge(gate_a, 3 * (h + 1))
                    nc.vector.scalar_tensor_tensor(lsA, lsA, 0.0, lsC, ALU.min, ALU.subtract).then_inc(gate_ls, 1)
                    v.wait_ge(gate_ls, h + 1)
                    nc.vector.tensor_scalar(lsA, lsA, 1.0 / TAU, None, ALU.mult).then_inc(gate_la, 1)
                    v.wait_ge(gate_la, h + 1)
                    g0 = cumg[:, h * SEQ:(h + 1) * SEQ]
                    g1 = cumg[:, (HEADS + h) * SEQ:(HEADS + h + 1) * SEQ]
                    nc.vector.tensor_tensor_scan(g0, reset, lsA[:, 0:SEQ], 0.0, ALU.mult, ALU.add).then_inc(scan_ok, 1)
                    nc.vector.tensor_tensor_scan(g1[:, ::-1], reset, lsA[:, SEQ:2 * SEQ][:, ::-1], 0.0, ALU.mult, ALU.add).then_inc(scan_ok, 1)
                v.wait_ge(dt_a, 2)
                nc.vector.tensor_scalar(u_, e_, 1.0, None, ALU.add).then_inc(dt_v, 1)
                v.wait_ge(dt_v, 3)
                nc.vector.scalar_tensor_tensor(dt_n, u_, -1.0, e_, ALU.add, ALU.subtract).then_inc(dt_v, 1)
                nc.vector.reciprocal(r_, u_).then_inc(dt_v, 1)
                v.wait_ge(dt_v, 5)
                nc.vector.tensor_tensor(dt_n, dt_n, r_, ALU.mult).then_inc(dt_v, 1)
                v.wait_ge(dt_v, 6)
                v.wait_ge(dt_a, 3)
                nc.vector.tensor_tensor(dt_n, l_, dt_n, ALU.subtract).then_inc(dt_v, 1)
                v.wait_ge(dt_v, 7)
                nc.vector.scalar_tensor_tensor(dt_n, z_, 0.0, dt_n, ALU.max, ALU.add).then_inc(dt_v, 1)
                v.wait_ge(dt_v, 8)
                nc.vector.scalar_tensor_tensor(a_, dt_n, -1.0, neg_a.unsqueeze(1).broadcast_to([P, NT, 64]), ALU.mult, ALU.mult).then_inc(dta_ok, 1)
                v.wait_ge(cum_ps, 1)
                nc.vector.tensor_copy(cum_n, ps[:, 2, 0:256].rearrange("p (t h) -> p t h", t=NT)).then_inc(cum_v, 1)
                v.wait_ge(cum_ps, 2)
                nc.vector.tensor_copy(tot_, ps[:, 3, 0:256].rearrange("p (t h) -> p t h", t=NT)).then_inc(cum_v, 1)
                v.wait_ge(cum_v, 2)
                nc.vector.tensor_tensor(s_, tot_, cum_n, ALU.subtract).then_inc(cum_v, 1)
                v.wait_ge(cum_ps, 3)
                nc.vector.tensor_copy(cum_T[0:64, :], ps[0:64, 2, :]).then_inc(cumT_ok, 1)
                v.wait_ge(dt_a, 5)
                nc.vector.tensor_tensor(dend_n, dend_n, dt_n, ALU.mult).then_inc(cum_v, 1)

            @block.tensor
            def _(pe):
                pe.wait_ge(par_in, 16 * 8)
                pe.wait_ge(masks, 1)
                nc.tensor.transpose(ps[:, 4, 0:N_PAR], par_rows[0:N_PAR, 0:P], ident[0:N_PAR, 0:N_PAR]).then_inc(par_T, 1)
                nr = (TAPS + 1) * NCT
                nc.tensor.transpose(ps[:, 5, 0:nr], par_rows[0:nr, P:2 * P], ident[0:nr, 0:nr]).then_inc(par_T, 1)
                pe.wait_ge(x_sc, NT)
                for c in range(NK):
                    if c >= 2:
                        pe.wait_ge(xT_v if c % 2 else xT_a, c // 2)
                    for t in range(NT):
                        last = nc.tensor.transpose(ps[:, 2 + c % 2, t * P:(t + 1) * P], xw3[:, t, c * P:(c + 1) * P], ident[:])
                    last.then_inc(xT_ps, 1)
                pe.wait_ge(xT_a, NK // 2)
                pe.wait_ge(xT_v, NK // 2)
                pe.wait_ge(small_in, 48)
                pe.wait_ge(zeroed, 4)
                for k in range(NK):
                    last = nc.tensor.matmul(ps[0:48, 0, :], wS3[:, k, 0:48], xnT[:, k, :], start=k == 0, stop=k == NK - 1)
                last.then_inc(proj_ready, 1)
                for t in range(NT):
                    for k in range(NK):
                        last = nc.tensor.matmul(ps[:, 1, t * 64:(t + 1) * 64], xnT[:, k, t * P:(t + 1) * P], wS3[:, k, 48:112],
                                                start=k == 0, stop=k == NK - 1)
                last.then_inc(proj_ready, 1)
                pe.wait_ge(proj_taken, 1)
                pe.wait_ge(fw_in, 32)
                pe.wait_ge(par_ok, 2)
                for h in range(HEADS):
                    if h >= 2:
                        pe.wait_ge(gate_z, 2 * (h - 1))
                    for d in range(2):
                        r = slice(32 * d, 32 * d + RANK)
                        last = nc.tensor.matmul(ps[:, 4 + 2 * (h % 2) + d, :], fw2[r, h * DK:(h + 1) * DK], lr_T[r, :],
                                                start=True, stop=True)
                    last.then_inc(gate_ps, 1)
                for n in range(6):
                    if n == 1:
                        pe.wait_ge(dt_v, 1)
                    head_piece(pe, 0, n)
                pe.wait_ge(dta_ok, 1)
                for t in range(NT):
                    for d, m in ((0, low), (1, high)):
                        c0 = t * 64 + d * SH
                        last = nc.tensor.matmul(ps[:, 2, c0:c0 + SH], m[:], a_[:, t, d * SH:(d + 1) * SH], start=True, stop=True)
                last.then_inc(cum_ps, 1)
                for t in range(NT):
                    last = nc.tensor.matmul(ps[:, 3, t * 64:(t + 1) * 64], ones[:], a_[:, t, :], start=True, stop=True)
                last.then_inc(cum_ps, 1)
                pe.wait_ge(cum_v, 1)
                for t in range(NT):
                    last = nc.tensor.transpose(ps[0:64, 2, t * P:(t + 1) * P], cum_n[:, t, :], ident[:])
                last.then_inc(cum_ps, 1)
        def o_at(c):
            t, half = divmod(c, KG)
            return slice(half * CH, (half + 1) * CH), 4 + t // 2, slice((t % 2) * DV, (t % 2 + 1) * DV)

        def gla_pe(pe, h, nxt):
            def piece(n):
                if nxt:
                    head_piece(pe, h + 1, n)
            piece(0)
            piece(1)

            def transposes(d):
                pe.wait_ge(g_qk, h * 8 + 4 * d + 4)
                if d:
                    pe.wait_ge(kd_ok, h * 2 + 1)
                elif not (isinstance(h, int) and h == 0):
                    pe.wait_ge(oT_ok, h * 2)
                for t in range(NT):
                    last = nc.tensor.transpose(ps[:, 3, t * P:(t + 1) * P], g_e[d][3][:, t * P:(t + 1) * P], ident[:])
                last.then_inc(kd_ps, 1)
            transposes(0)
            pe.wait_ge(g_qk, h * 8 + 8)
            for d in range(2):
                for c in range(NCH):
                    rows = o_at(c)[0]
                    at = d * 4 * CH + (c // KG) * CH
                    i = slice(c * CH, (c + 1) * CH)
                    last = nc.tensor.matmul(ps[rows, 2, at:at + CH], g_e[d][1][:, i], g_e[d][0][:, i], start=True, stop=True)
            last.then_inc(s_ps, 1)
            piece(2)
            piece(3)
            transposes(1)
            piece(4)
            pe.wait_ge(s_sel, h * 2 + 2)
            pe.wait_ge(v_kept, h + 1)
            if not (isinstance(h, int) and h == 0):
                pe.wait_ge(o_v, h * 6)
            alone(pe)
            for c in range(NCH):
                rows, b, cols = o_at(c)
                nc.tensor.matmul(ps[rows, b, cols], s_w[rows, (c // KG) * CH:(c // KG + 1) * CH], v_w[rows, c // KG, :],
                                 start=(c // KG) % 2 == 0, stop=False, skip_group_check=True)
            pe.wait_ge(kd_ok, h * 2 + 2)
            for s in range(NCH):
                for d in range(2):
                    c = (s, NCH - 1 - s)[d]
                    rows, b, cols = o_at(c)
                    if s:
                        pe.wait_ge(st_ok, h * 14 + 2 * (s - 1) + d + 1)
                        last = nc.tensor.matmul(ps[rows, b, cols], g_e[d][2][:, c * CH:(c + 1) * CH], g_st[d],
                                                start=False, stop=s == max(c, NCH - 1 - c), skip_group_check=True)
                    if s < NCH - 1:
                        nc.tensor.matmul(ps[:, 6 + d, 0:DV], kd_n[rows, d, c // KG, :], v_w[rows, c // KG, :],
                                         start=True, stop=True).then_inc(st_ps, 1)
                if s in (1, 3):
                    piece(5 + s // 2)
            last.then_inc(o_ps, 1)
            piece(7)
            pe.wait_ge(o_v, h * 6 + 6)
            for j in range(2):
                for t in range(NT):
                    last = nc.tensor.transpose(ps[:, 3 - j, t * P:(t + 1) * P], o_n[:, t, j * P:(j + 1) * P], ident[:])
                last.then_inc(oT_ps, 1)

        def gla_act(act, h, nxt):
            def take_tile(n):
                if nxt:
                    head_take(act, h + 1, n)
            first = isinstance(h, int) and h == 0
            for d in range(2):
                for i in range(4):
                    if i == 0:
                        act.wait_ge(g_diff, h * 4 + 2 * d + 2)
                        if not first:
                            act.wait_ge(o_ps, h)
                    src = g_d[d][0] if i < 2 else g_d[d][1] if i == 3 else cumg[:, bass.ds(h * SEQ + d * HEADS * SEQ, SEQ)]
                    nc.scalar.activation(g_e[d][i], src, ACT.Exp, scale=-1.0 if i == 1 else 1.0).then_inc(g_exp, 1)
            take_tile(0)
            take_tile(1)

            def keep_kd(d):
                act.wait_ge(kd_ps, h * 2 + d + 1)
                nc.scalar.activation(kd_n[:, d], ps[:, 3, :].rearrange("p (t n) -> p t n", t=NT), ACT.Copy).then_inc(kd_ok, 1)
            keep_kd(0)
            take_tile(2)
            take_tile(3)
            keep_kd(1)
            take_tile(4)
            take_tile(5)
            take_tile(6)
            act.wait_ge(o_ps, h + 1)
            for t in range(NT):
                if t or not first:
                    act.wait_ge(o_sq, h * 5 + t)
                nc.scalar.activation(o_junk, ps[:, 4 + t // 2, (t % 2) * DV:(t % 2 + 1) * DV], ACT.Square,
                                     accum_out=stat[:, 16 + t:17 + t]).then_inc(o_sq, 1)
            act.wait_ge(o_v, h * 6 + 1)
            nc.scalar.activation(stat[:, 24:28], stat[:, 20:24], ACT.Sqrt).then_inc(o_sq, 1)
            take_tile(7)

        def gla_pool(pool, h):
            pool.wait_ge(hp_taken, h * 8 + 6)
            if not (isinstance(h, int) and h == 0):
                pool.wait_ge(o_ps, h)
            alone(pool)
            nc.gpsimd.tensor_copy(v_w, v_raw).then_inc(v_kept, 1)
            pool.wait_ge(hp_taken, h * 8 + 8)
            if not (isinstance(h, int) and h == 0):
                pool.wait_ge(oT_ok, h * 2)
            alone(pool)
            nc.gpsimd.tensor_copy(r_w, r_raw).then_inc(r_kept, 1)

        def gla_dve(v, h):
            first = isinstance(h, int) and h == 0
            for d in range(2):
                b = cumg[:, bass.ds(h * SEQ + d * HEADS * SEQ, SEQ)]
                b3 = by_chunk(b)
                if not first:
                    v.wait_ge(g_exp, h * 8)
                for i, at in enumerate((MID[d], LAST[d])):
                    edge = b3[:, :, at:at + 1].broadcast_to([P, NCH, CH])
                    o, s = (b3, edge) if i == 0 else (edge, b3)
                    nc.vector.tensor_tensor(by_chunk(g_d[d][i]), o, s, ALU.subtract).then_inc(g_diff, 1)
            v.wait_ge(hp_taken, h * 8 + 2)
            for d in range(2):
                v.wait_ge(g_exp, h * 8 + 4 * d + 3)
                if not first:
                    v.wait_ge(st_ok, h * 14)
                nc.vector.tensor_copy(dec[:, d, :].unsqueeze(2), by_chunk(g_e[d][2])[:, :, LAST[d]:LAST[d] + 1]).then_inc(g_dec, 1)
                v.wait_ge(g_dec, h * 2 + d + 1)
                v.wait_ge(g_exp, h * 8 + 4 * d + 4)
                for i, raw in enumerate((q_raw, k_raw, q_raw, k_raw)):
                    nc.vector.tensor_tensor(g_e[d][i], g_e[d][i], raw, ALU.mult).then_inc(g_qk, 1)
            v.wait_ge(s_ps, h + 1)
            if not first:
                v.wait_ge(s_sel, h * 2)
            alone(v)
            nc.vector.copy_predicated(s_m, gmask.bitcast(U32), ps[:, 2, :]).then_inc(s_sel, 1)
            v.wait_ge(s_sel, h * 2 + 1)
            nc.vector.tensor_tensor(s_w, s_m[:, 0:SEQ // 2], s_m[:, SEQ // 2:SEQ], ALU.add).then_inc(s_sel, 1)
            for s in range(NCH - 1):
                for d in range(2):
                    c = (s, NCH - 1 - s)[d]
                    v.wait_ge(st_ps, h * 14 + 2 * s + d + 1)
                    if s == 0:
                        if not first:
                            v.wait_ge(st_ok, h * 14)
                        nc.vector.tensor_copy(g_st[d], ps[:, 6 + d, 0:DV]).then_inc(st_ok, 1)
                    else:
                        v.wait_ge(st_ok, h * 14 + 2 * (s - 1) + d + 1)
                        nc.vector.scalar_tensor_tensor(g_st[d], g_st[d], dec[:, d, c:c + 1], ps[:, 6 + d, 0:DV],
                                                       ALU.mult, ALU.add).then_inc(st_ok, 1)
            v.wait_ge(o_sq, h * 5 + 4)
            nc.vector.tensor_scalar(stat[:, 20:24], stat[:, 16:20], 1.0 / DV, EPS, ALU.mult, ALU.add).then_inc(o_v, 1)
            v.wait_ge(o_sq, h * 5 + 5)
            nc.vector.reciprocal(stat[:, 28:32], stat[:, 24:28]).then_inc(o_v, 1)
            v.wait_ge(o_v, h * 6 + 2)
            for t in range(NT):
                nc.vector.tensor_scalar(o_n[:, t, :], ps[:, 4 + t // 2, (t % 2) * DV:(t % 2 + 1) * DV],
                                        stat[:, 28 + t:29 + t], None, ALU.mult).then_inc(o_v, 1)
            v.wait_ge(r_kept, h + 1)
            for j in range(2):
                v.wait_ge(oT_ps, h * 2 + j + 1)
                dst = oT.rearrange("p c t -> p (c t)")[:, bass.ds(h * 2 * SEQ + j * SEQ, SEQ)]
                nc.vector.scalar_tensor_tensor(dst, ps[:, 3 - j, :], par[:, R_GLA + j:R_GLA + j + 1], r_w[:, j, :],
                                               ALU.mult, ALU.mult).then_inc(oT_ok, 1)

        with nc.Block() as block:
            @block.sync
            def _(sp):
                with sp.Fori(1, HEADS) as h:
                    sp.wait_ge(hp_ready, h * 8 - 6)
                    load_head(sp, h)
                    sp.wait_ge(hp_ready, h * 8 - 2)
                    load_head_v(sp, h)
                    sp.wait_ge(hp_ready, h * 8)
                    load_head_r(sp, h)

            @block.tensor
            def _(pe):
                for n in range(6, 8):
                    head_piece(pe, 0, n)
                gla_pe(pe, 0, True)
                with pe.Fori(1, HEADS - 1) as h:
                    gla_pe(pe, h, True)
                gla_pe(pe, HEADS - 1, False)

            @block.scalar
            def _(act):
                for n in range(6, 8):
                    head_take(act, 0, n)
                gla_act(act, 0, True)
                with act.Fori(1, HEADS - 1) as h:
                    gla_act(act, h, True)
                gla_act(act, HEADS - 1, False)

            @block.gpsimd
            def _(pool):
                gla_pool(pool, 0)
                with pool.Fori(1, HEADS) as h:
                    gla_pool(pool, h)

            @block.vector
            def _(v):
                nc.vector.memset(s_m, 0.0).then_inc(pads, 1)
                v.wait_ge(pads, 1)
                gla_dve(v, 0)
                with v.Fori(1, HEADS) as h:
                    gla_dve(v, h)

        gp_ready = sem("gp_ready")
        gp_taken = sem("gp_taken")
        z_ok = sem("z_ok")
        cv_par = sem("cv_par")
        cv_first = sem("cv_first")
        cv_taps = sem("cv_taps")
        cv_silu = sem("cv_silu")
        xn_ps = sem("xn_ps")
        xn_ok = sem("xn_ok")
        cb_ps = sem("cb_ps")
        cb_ok = sem("cb_ok")
        bc_cum = sem("bc_cum")
        seg = sem("seg")
        seg_min = sem("seg_min")
        seg_exp = sem("seg_exp")
        m_ok = sem("m_ok")
        xdt_ok = sem("xdt_ok")
        xd_ok = sem("xd_ok")
        yi_ps = sem("yi_ps")
        yi_ok = sem("yi_ok")
        xe_ok = sem("xe_ok")
        su_ps = sem("su_ps")
        in_ps = sem("in_ps")
        in_ok = sem("in_ok")
        ya_ok = sem("ya_ok")
        sd_ok = sem("sd_ok")
        ss_ok = sem("ss_ok")
        yz_ok = sem("yz_ok")
        y_sq = sem("y_sq")
        yn_ok = sem("yn_ok")
        yT_ps = sem("yT_ps")
        yT_ok = sem("yT_ok")
        y_out = sem("y_out")

        take_anew()
        CTG = 6
        WID = SEQ + TAPS - 1
        x_raw = take(CTG * WID).rearrange("p (c t) -> p c t", c=CTG)
        z_raw, z_w = (take_side(NT * GW).rearrange("p (t n) -> p t n", t=NT) for _ in range(2))
        xcT = take(CTG * SEQ).rearrange("p (c t) -> p c t", c=CTG)
        yT_w = xcT[:, 0:4, :]
        b_n = take_side(SEQ).rearrange("p (t n) -> p t n", t=NT)
        x_n, y_n = (take_side(NT * GW).rearrange("p (t n) -> p t n", t=NT) for _ in range(2))
        s_st = [take(GW) for _ in range(2)]
        x_dt = [[take(GW) for _ in range(2)], s_st]
        x_e = [take_side(GW) for _ in range(2)]
        cum_bc = [a.rearrange("p (d h i) -> p d h i", d=2, h=HPG) for a in
                  (take(UNIT), take(UNIT), weights[:, UNIT:2 * UNIT], weights[:, 2 * UNIT:3 * UNIT])]
        m_w = [[a[:, d * HPG * P:(d + 1) * HPG * P].rearrange("p (h i) -> p h i", h=HPG) for d in range(2)]
               for a in (take(UNIT), weights[:, 0:UNIT])]
        cb_m = [take(SEQ).rearrange("p (t i) -> p t i", t=NT) for _ in range(2)]
        x_D = x_e
        in_w = x_dt[0]
        cvp = take(CTG * (TAPS + 1)).rearrange("p (k c) -> p k c", c=CTG)
        gain = take(4)

        def by_head(ap):
            return ap.rearrange("p (h n) -> p h n", h=HPG)

        def per_head(i, t, g, d):
            flat = dt_all[:, bass.ds(g * HPG + (i * NT * 64 + t * 64 + d * SH), HPG)]
            return flat.unsqueeze(2).broadcast_to([P, HPG, HD])

        def per_head_i(i, t, g, d):
            flat = dt_all[:, bass.ds(g * HPG + (i * NT * 64 + t * 64 + d * SH), HPG)]
            return flat.unsqueeze(2).broadcast_to([P, HPG, P])

        DT, CUM, ECUM, DEND, ETOT = range(5)

        def is_first(g):
            return isinstance(g, int) and g == 0

        def group_piece(pe, g, n):
            if not (is_first(g) and n < 2):
                pe.wait_ge(gp_taken, g * 10 + n - 1)
            w = {0: 3, 4: 0, 6: 1, 8: 2}.get(n)
            if w is not None:
                pe.wait_ge(group_w[w], (g + 1) * (32 if w == 2 else 16))
                if w == 3:
                    pe.wait_ge(group_w[4], (g + 1) * 16)
            b = n % 2
            if n < 4:
                for j in range(2):
                    for k in range(NK):
                        last = nc.tensor.matmul(ps[:, b, j * 256:(j + 1) * 256], xnT[:, k, n * P:(n + 1) * P],
                                                slot(6 + j, NK)[:, k, :], start=k == 0, stop=k == NK - 1)
            else:
                c = n - 4
                for k in range(NK):
                    last = nc.tensor.matmul(ps[:, b, :], slot(3 + c // 2, NK)[:, k, (c % 2) * P:(c % 2 + 1) * P], xnT[:, k, :],
                                            start=k == 0, stop=k == NK - 1)
            last.then_inc(gp_ready, 1)

        def group_take(act, g, n):
            act.wait_ge(gp_ready, g * 10 + n + 1)
            b = n % 2
            if n < 4:
                if n == 0 and not is_first(g):
                    act.wait_ge(z_ok, g)
                nc.scalar.activation(z_raw[:, n, :], ps[:, b, :], ACT.Copy).then_inc(gp_taken, 1)
            else:
                if n == 4:
                    if is_first(g):
                        act.wait_ge(pads, 3)
                    else:
                        act.wait_ge(cv_taps, g * 18)
                nc.scalar.activation(x_raw[:, n - 4, 1:1 + SEQ], ps[:, b, :], ACT.Copy).then_inc(gp_taken, 1)

        def ssd_pe(pe, g, nxt):
            def piece(n):
                if nxt:
                    group_piece(pe, g + 1, n)
            piece(0)
            piece(1)
            piece(2)
            for i in range(5):
                if i == 0:
                    pe.wait_ge(cv_silu, g * 6 + 4)
                    if not is_first(g):
                        pe.wait_ge(in_ok, g * 6)
                elif i == 4:
                    pe.wait_ge(cv_silu, g * 6 + 6)
                if i >= 2:
                    pe.wait_ge(xn_ok, g * 5 + i - 1)
                for c in range(4):
                    src = xcT[:, c, i * P:(i + 1) * P] if i < 4 else xcT[:, 4, c * P:(c + 1) * P]
                    last = nc.tensor.transpose(ps[:, 2 + i % 2, c * P:(c + 1) * P], src, ident[:])
                last.then_inc(xn_ps, 1)
            pe.wait_ge(xn_ok, g * 5 + 4)
            for t in range(NT):
                i = slice(t * P, (t + 1) * P)
                last = nc.tensor.matmul(ps[:, 3, i], xcT[:, 4, i], xcT[:, 5, i], start=True, stop=True)
            last.then_inc(cb_ps, 1)
            piece(3)
            for t in range(NT):
                pe.wait_ge(m_ok, g * 8 + 2 * t + 2)
                pe.wait_ge(xdt_ok, g * 8 + 2 * t + 2)
                if t >= 2:
                    pe.wait_ge(yi_ok, g * 4 + t - 1)
                elif not is_first(g):
                    pe.wait_ge(yT_ok, g * 4)
                for h in range(HPG):
                    for d in range(2):
                        last = nc.tensor.matmul(ps[:, 4 + t % 2, h * HD:(h + 1) * HD], m_w[t % 2][d][:, h, :],
                                                x_dt[t % 2][d][:, h * HD:(h + 1) * HD], start=d == 0, stop=d == 1)
                last.then_inc(yi_ps, 1)
                if t < 3:
                    piece(4 + t)
            for s in range(NT):
                for d in range(2):
                    t = (s, NT - 1 - s)[d]
                    if s:
                        pe.wait_ge(ss_ok, g * 6 + 2 * (s - 1) + d + 1)
                        if s > 1:
                            pe.wait_ge(in_ok, g * 6 + 2 * (s - 2) + d + 1)
                        else:
                            pe.wait_ge(cb_ok, g * 2 + 2)
                            pe.wait_ge(xn_ok, g * 5 + 5)
                        nc.tensor.matmul(ps[:, 2 + d, :], xcT[:, 5, t * P:(t + 1) * P], s_st[d], start=True, stop=True).then_inc(in_ps, 1)
                    if s < NT - 1:
                        pe.wait_ge(xe_ok, g * 6 + 2 * s + d + 1)
                        if s == 0 and not is_first(g):
                            pe.wait_ge(ss_ok, g * 6)
                        nc.tensor.matmul(ps[:, 6 + d, :], b_n[:, t, :], x_e[d], start=True, stop=True).then_inc(su_ps, 1)
                if s in (0, 1, 3):
                    piece({0: 7, 1: 8, 3: 9}[s])
            for c in range(4):
                pe.wait_ge(yn_ok, g * 6 + 6)
                if c >= 2:
                    pe.wait_ge(yT_ok, g * 4 + c - 1)
                for t in range(NT):
                    last = nc.tensor.transpose(ps[:, 4 + c % 2, t * P:(t + 1) * P], y_n[:, t, c * P:(c + 1) * P], ident[:])
                last.then_inc(yT_ps, 1)

        def ssd_act(act, g, nxt):
            def take_tile(n):
                if nxt:
                    group_take(act, g + 1, n)
            act.wait_ge(cv_par, g * 4 + 3)
            act.wait_ge(gp_taken, g * 10 + 10)
            for c in range(CTG):
                if not is_first(g):
                    if c == 0:
                        act.wait_ge(y_out, g * 16)
                    if c == 4:
                        act.wait_ge(in_ps, g * 6)
                nc.scalar.activation(xcT[:, c, :], x_raw[:, c, 1:1 + SEQ], ACT.Identity, scale=cvp[:, 1, c:c + 1],
                                     bias=cvp[:, TAPS, c:c + 1]).then_inc(cv_first, 1)
            act.wait_ge(gp_taken, g * 10 + 4)
            if not is_first(g):
                act.wait_ge(yz_ok, g * 4)
            nc.scalar.activation(z_w, z_raw, ACT.Silu).then_inc(z_ok, 1)
            take_tile(0)
            for c in range(CTG):
                act.wait_ge(cv_taps, g * 18 + 3 * c + 3)
                nc.scalar.activation(xcT[:, c, :], xcT[:, c, :], ACT.Silu).then_inc(cv_silu, 1)
            take_tile(1)
            take_tile(2)
            for i in range(5):
                act.wait_ge(xn_ps, g * 5 + i + 1)
                if i == 0 and not is_first(g):
                    act.wait_ge(xe_ok, g * 6)
                    act.wait_ge(su_ps, g * 6)
                    act.wait_ge(xd_ok, g * 4)
                dst = x_n[:, i, :] if i < 4 else b_n.rearrange("p t n -> p (t n)")
                nc.scalar.activation(dst, ps[:, 2 + i % 2, :], ACT.Copy).then_inc(xn_ok, 1)
            for t in range(NT):
                act.wait_ge(seg_min, g * 4 + t + 1)
                e = cum_bc[t][:, 0]
                nc.scalar.activation(e, e, ACT.Exp).then_inc(seg_exp, 1)
                if t:
                    take_tile(2 + t)
            for n in (6, 7, 8):
                take_tile(n)
            for t in range(NT):
                act.wait_ge(yz_ok, g * 4 + t + 1)
                if t or not is_first(g):
                    act.wait_ge(y_sq, g * 5 + t)
                nc.scalar.activation(x_e[0], y_n[:, t, :], ACT.Square, accum_out=stat[:, 32 + t:33 + t]).then_inc(y_sq, 1)
            act.wait_ge(yn_ok, g * 6 + 1)
            nc.scalar.activation(stat[:, 40:44], stat[:, 36:40], ACT.Sqrt).then_inc(y_sq, 1)
            take_tile(9)
            act.wait_ge(cv_par, g * 4 + 4)
            for c in range(4):
                act.wait_ge(yT_ps, g * 4 + c + 1)
                nc.scalar.activation(yT_w[:, c, :], ps[:, 4 + c % 2, :], ACT.Copy, scale=gain[:, c:c + 1]).then_inc(yT_ok, 1)

        def load_cum(sp, g):
            for t in range(NT):
                src = cum_d.rearrange("t g d h i -> t (g d h i)")[t:t + 1, bass.ds(g * 2 * HPG * P, 2 * HPG * P)]
                sp.dma_start(cum_bc[t].rearrange("p d h i -> p (d h i)"), src.broadcast_to([P, 2 * HPG * P])).then_inc(bc_cum, 16)

        def ssd_pool(pool, g):
            pool.wait_ge(bc_cum, g * 64 + 64)
            for t in range(NT):
                for d in range(2):
                    b = cum_bc[t][:, d]
                    alone(pool)
                    nc.gpsimd.tensor_tensor(b, b, per_head_i(CUM, t, g, d), ALU.subtract).then_inc(seg, 1)
            for t in range(NT):
                pool.wait_ge(xn_ok, g * 5 + t + 1)
                if t >= 2:
                    pool.wait_ge(yi_ok, g * 4 + t - 1)
                elif not is_first(g):
                    pool.wait_ge(y_sq, g * 5)
                alone(pool)
                dh = d_bc[:, bass.ds(g * HPG, HPG)].unsqueeze(2).broadcast_to([P, HPG, HD])
                nc.gpsimd.tensor_tensor(by_head(x_D[t % 2]), by_head(x_n[:, t, :]), dh, ALU.mult).then_inc(xd_ok, 1)
            for s in range(1, NT):
                for d in range(2):
                    t = (s, NT - 1 - s)[d]
                    if s < NT - 1:
                        pool.wait_ge(in_ps, g * 6 + 2 * (s - 1) + d + 1)
                        pool.wait_ge(ss_ok, g * 6 + 2 * (s - 1) + d + 1)
                        alone(pool)
                        nc.gpsimd.tensor_tensor(by_head(s_st[d]), by_head(s_st[d]), per_head(ETOT, t, g, d), ALU.mult).then_inc(sd_ok, 1)
                for d in range(2):
                    t = (s, NT - 1 - s)[d]
                    pool.wait_ge(in_ok, g * 6 + 2 * (s - 1) + d + 1)
                    pool.wait_ge(yi_ok, g * 4 + 4)
                    if s > 1:
                        pool.wait_ge(ya_ok, g * 6 + 2 * (s - 1))
                    alone(pool)
                    nc.gpsimd.tensor_tensor(y_n[:, t, :], y_n[:, t, :], in_w[d], ALU.add).then_inc(ya_ok, 1)

        def ssd_dve(v, g):
            if not is_first(g):
                v.wait_ge(yT_ok, g * 4)
                v.wait_ge(cv_first, g * 6)
                v.wait_ge(cv_taps, g * 18)
            cp3 = conv_par[:, :].rearrange("p (k c) -> p k c", k=TAPS + 1)
            nc.vector.tensor_copy(cvp[:, :, 0:4], cp3[:, :, bass.ds(g * 4, 4)]).then_inc(cv_par, 1)
            nc.vector.tensor_copy(cvp[:, :, 4:5], cp3[:, :, bass.ds(g + 16, 1)]).then_inc(cv_par, 1)
            nc.vector.tensor_copy(cvp[:, :, 5:6], cp3[:, :, bass.ds(g + 20, 1)]).then_inc(cv_par, 1)
            nc.vector.tensor_copy(gain, par[:, bass.ds(g * 4 + R_SSD, 4)]).then_inc(cv_par, 1)
            v.wait_ge(cv_par, g * 4 + 3)
            for c in range(CTG):
                v.wait_ge(cv_first, g * 6 + c + 1)
                for i, k in enumerate((0, 2, 3)):
                    if i:
                        v.wait_ge(cv_taps, g * 18 + 3 * c + i)
                    nc.vector.scalar_tensor_tensor(xcT[:, c, :], x_raw[:, c, k:k + SEQ], cvp[:, k, c:c + 1], xcT[:, c, :],
                                                   ALU.mult, ALU.add).then_inc(cv_taps, 1)

            def seg_least(t):
                v.wait_ge(seg, g * 8 + 2 * t + 2)
                b = cum_bc[t]
                nc.vector.tensor_tensor(b[:, 0], b[:, 0], b[:, 1], ALU.min).then_inc(seg_min, 1)

            def x_by_dt(t):
                v.wait_ge(xn_ok, g * 5 + t + 1)
                if t >= 2:
                    v.wait_ge(yi_ps, g * 4 + t - 1)
                for d in range(2):
                    nc.vector.tensor_tensor(by_head(x_dt[t % 2][d]), by_head(x_n[:, t, :]), per_head(DT, t, g, d), ALU.mult).then_inc(xdt_ok, 1)

            def y_begin(t):
                v.wait_ge(yi_ps, g * 4 + t + 1)
                v.wait_ge(xd_ok, g * 4 + t + 1)
                nc.vector.tensor_tensor(y_n[:, t, :], ps[:, 4 + t % 2, :], x_D[t % 2], ALU.add).then_inc(yi_ok, 1)

            seg_least(0)
            x_by_dt(0)
            v.wait_ge(cb_ps, g + 1)
            for d, m in ((0, low), (1, high)):
                nc.vector.tensor_tensor(cb_m[d], ps[:, 3, :].rearrange("p (t i) -> p t i", t=NT),
                                        m[:].unsqueeze(1).broadcast_to([P, NT, P]), ALU.mult).then_inc(cb_ok, 1)
            for t in range(NT):
                if t + 1 < NT:
                    seg_least(t + 1)
                v.wait_ge(seg_exp, g * 4 + t + 1)
                v.wait_ge(cb_ok, g * 2 + 2)
                if t >= 2:
                    v.wait_ge(yi_ps, g * 4 + t - 1)
                for d in range(2):
                    nc.vector.tensor_tensor(m_w[t % 2][d], cum_bc[t][:, 0], cb_m[d][:, t, :].unsqueeze(1).broadcast_to([P, HPG, P]),
                                            ALU.mult).then_inc(m_ok, 1)
                if t + 1 < NT:
                    x_by_dt(t + 1)
                if t:
                    y_begin(t - 1)
            y_begin(NT - 1)
            for s in range(NT):
                if s < NT - 1:
                    for d in range(2):
                        t = (s, NT - 1 - s)[d]
                        if s:
                            v.wait_ge(su_ps, g * 6 + 2 * (s - 1) + d + 1)
                        else:
                            v.wait_ge(yi_ok, g * 4 + 4)
                        nc.vector.tensor_tensor(by_head(x_e[d]), by_head(x_n[:, t, :]), per_head(DEND, t, g, d), ALU.mult).then_inc(xe_ok, 1)
                if s:
                    for d in range(2):
                        t = (s, NT - 1 - s)[d]
                        v.wait_ge(in_ps, g * 6 + 2 * (s - 1) + d + 1)
                        v.wait_ge(yi_ok, g * 4 + 4)
                        if s > 1:
                            v.wait_ge(ya_ok, g * 6 + 2 * (s - 1))
                        nc.vector.tensor_tensor(by_head(in_w[d]), by_head(ps[:, 2 + d, :]), per_head(ECUM, t, g, d), ALU.mult).then_inc(in_ok, 1)
                if s < NT - 1:
                    for d in range(2):
                        v.wait_ge(su_ps, g * 6 + 2 * s + d + 1)
                        if s:
                            v.wait_ge(sd_ok, g * 4 + 2 * (s - 1) + d + 1)
                            nc.vector.tensor_tensor(s_st[d], s_st[d], ps[:, 6 + d, :], ALU.add).then_inc(ss_ok, 1)
                        else:
                            if not is_first(g):
                                v.wait_ge(in_ps, g * 6)
                            nc.vector.tensor_copy(s_st[d], ps[:, 6 + d, :]).then_inc(ss_ok, 1)
            v.wait_ge(ya_ok, g * 6 + 6)
            v.wait_ge(z_ok, g + 1)
            for t in range(NT):
                nc.vector.tensor_tensor(y_n[:, t, :], y_n[:, t, :], z_w[:, t, :], ALU.mult).then_inc(yz_ok, 1)
            v.wait_ge(y_sq, g * 5 + 4)
            nc.vector.tensor_scalar(stat[:, 36:40], stat[:, 32:36], 1.0 / GW, EPS, ALU.mult, ALU.add).then_inc(yn_ok, 1)
            v.wait_ge(y_sq, g * 5 + 5)
            nc.vector.reciprocal(stat[:, 44:48], stat[:, 40:44]).then_inc(yn_ok, 1)
            v.wait_ge(yn_ok, g * 6 + 2)
            for t in range(NT):
                nc.vector.tensor_scalar(y_n[:, t, :], y_n[:, t, :], stat[:, 44 + t:45 + t], None, ALU.mult).then_inc(yn_ok, 1)

        def load_group(sp, g):
            sp.wait_ge(gp_ready, g * 10 - 6)
            load_group_z(sp, g, 0)
            load_group_z(sp, g, 1)
            sp.wait_ge(gp_ready, g * 10 - 4)
            load_group_x(sp, g, 0)
            sp.wait_ge(gp_ready, g * 10 - 2)
            load_group_x(sp, g, 1)
            if not (isinstance(g, int) and g == 1):
                sp.wait_ge(m_ok, g * 8 - 8)
                load_cum(sp, g - 1)
            sp.wait_ge(gp_ready, g * 10)
            load_group_bc(sp, g)

        def store_y(sp, g):
            sp.wait_ge(yT_ok, g * 4 + 4)
            flat = y_d.rearrange("g p n -> p g n")
            sp.dma_start(flat[:, bass.ds(g, 1), :].rearrange("p g n -> p (g n)"), yT_w.rearrange("p c t -> p (c t)")).then_inc(y_out, 16)

        with nc.Block() as block:
            @block.sync
            def _(sp):
                load_cum(sp, 0)
                load_group(sp, 1)
                with sp.Fori(2, GR) as g:
                    load_group(sp, g)
                    store_y(sp, g - 2)
                sp.wait_ge(m_ok, 8 * (GR - 1))
                load_cum(sp, GR - 1)
                sp.wait_ge(gp_ready, 10 * GR)
                load_mix(sp, 0, 3)
                load_mix(sp, 0, 4)
                for n in range(3):
                    load_out(sp, n)
                store_y(sp, GR - 2)
                sp.wait_ge(yi_ps, NT * GR)
                for s in range(3):
                    load_mix(sp, 0, s)
                store_y(sp, GR - 1)
                sp.wait_ge(y_out, 16 * GR)

            @block.tensor
            def _(pe):
                for n in range(10):
                    group_piece(pe, 0, n)
                ssd_pe(pe, 0, True)
                with pe.Fori(1, GR - 1) as g:
                    ssd_pe(pe, g, True)
                ssd_pe(pe, GR - 1, False)

            @block.scalar
            def _(act):
                for n in range(10):
                    group_take(act, 0, n)
                ssd_act(act, 0, True)
                with act.Fori(1, GR - 1) as g:
                    ssd_act(act, g, True)
                ssd_act(act, GR - 1, False)

            @block.gpsimd
            def _(pool):
                ssd_pool(pool, 0)
                with pool.Fori(1, GR) as g:
                    ssd_pool(pool, g)

            @block.vector
            def _(v):
                nc.vector.memset(x_raw[:, :, 0:1], 0.0).then_inc(pads, 1)
                nc.vector.memset(x_raw[:, :, 1 + SEQ:WID], 0.0).then_inc(pads, 1)
                ssd_dve(v, 0)
                with v.Fori(1, GR) as g:
                    ssd_dve(v, g)

        gf_in = sem("gf_in")
        mx_ps = sem("mx_ps")
        mx_sg = sem("mx_sg")
        mx_pr = sem("mx_pr")
        mx_ok = sem("mx_ok")
        h_ps = sem("h_ps")
        h_ok = sem("h_ok")
        h_sq = sem("h_sq")
        h_v = sem("h_v")
        f_out = sem("f_out")
        fT_ps = sem("fT_ps")
        fT_ok = sem("fT_ok")
        lg_ps = sem("lg_ps")
        b_in = sem("b_in")
        b1_ps = sem("b1_ps")
        b1_ok = sem("b1_ok")

        take_anew()
        yT = take_side(DIN // P * SEQ).rearrange("p (c t) -> p c t", c=DIN // P)
        mixT_f = take(NK * SEQ)
        mixT = mixT_f.rearrange("p (c t) -> p c t", c=NK)
        gates_w = [[take(SEQ) for _ in range(2)] for _ in range(2)]
        h3 = T[:, TEMPS - NT * D:TEMPS].rearrange("p (t d) -> p t d", t=NT)
        gf_bc = take_side(D)
        b1_rows = take_side(4 * P).rearrange("p (a c) -> p a c", a=4)
        f_n = yT.rearrange("p c t -> p (c t)")[:, 0:NT * D].rearrange("p (t d) -> p t d", t=NT)
        f_T = yT.rearrange("p c t -> p (c t)")[:, NT * D:2 * NT * D].rearrange("p (c t) -> p c t", c=NK)
        wr_w = take(NK * NE).rearrange("p (k n) -> p k n", k=NK)
        lg = take(NT * NE).rearrange("p (t e) -> p t e", t=NT)

        def mix_pe(pe, i):
            for m in range(2):
                for n, (w, src) in enumerate((((0,), xnT), ((1,), xnT), ((2,), oT), ((3, 4), yT))):
                    if m == 0:
                        for s in w:
                            pe.wait_ge(mix_w[s], (i + 1) * 16)
                        if n == 3 and is_first(i):
                            pe.wait_ge(y_out, 32 * GR)
                    if not is_first(i):
                        pe.wait_ge(mx_pr, i * 4 - 2 + 2 * m if n >= 2 else i * 4 - 2 + 2 * m)
                    cnt = len(w) * NK
                    for k in range(cnt):
                        last = nc.tensor.matmul(ps[:, 4 * m + n, :], slot(w[k // NK], NK)[:, k % NK, m * P:(m + 1) * P], src[:, k, :],
                                                start=k == 0, stop=k == cnt - 1)
                    last.then_inc(mx_ps, 1)

        with nc.Block() as block:
            @block.sync
            def _(sp):
                for g in range(GR):
                    sp.dma_start(yT[:, 4 * g:4 * g + 4, :].rearrange("p c t -> p (c t)"), y_d[g]).then_inc(y_out, 16)
                for t in range(NT):
                    sp.dma_start(h3[:, t, :], x[t * P:(t + 1) * P, :]).then_inc(x_in, 16)
                sp.dma_start(gf_bc, norm_ffn_g.rearrange("(a n) -> a n", a=1).broadcast_to([P, D])).then_inc(gf_in, 16)
                sp.dma_start(wr_w, w_router.rearrange("(k p) n -> p k n", p=P)).then_inc(gf_in, 16)
                sp.dma_start(b1_rows, b1.rearrange("(a e) (j c) -> e j a c", a=4, c=P).rearrange("e j a c -> (e j) a c")).then_inc(b_in, 16)
                with sp.Fori(1, 4) as i:
                    sp.wait_ge(mx_ps, i * 8 - 3)
                    alone(sp)
                    load_mix(sp, i, 0)
                    sp.wait_ge(mx_ps, i * 8 - 2)
                    alone(sp)
                    load_mix(sp, i, 1)
                    sp.wait_ge(mx_ps, i * 8 - 1)
                    alone(sp)
                    load_mix(sp, i, 2)
                    sp.wait_ge(mx_ps, i * 8)
                    alone(sp)
                    load_mix(sp, i, 3)
                    load_mix(sp, i, 4)
                sp.wait_ge(mx_ps, 32 - 3)
                load_out(sp, 3)
                sp.wait_ge(mx_ps, 32)
                for u in (1, 2, 3, 4, 8, 9, 10, 11):
                    load_expert(sp, 0, u)
                sp.wait_ge(h_ps, NT)
                for u in (0, 5, 6, 7):
                    load_expert(sp, 0, u)
                for t in range(NT):
                    sp.wait_ge(h_v, 3 + t)
                    sp.dma_start(xn_d[t * P:(t + 1) * P, :], f_n[:, t, :]).then_inc(f_out, 16)
                sp.wait_ge(f_out, 16 * NT)

            @block.tensor
            def _(pe):
                mix_pe(pe, 0)
                with pe.Fori(1, 4) as i:
                    mix_pe(pe, i)
                pe.wait_ge(mx_ok, 8)
                for t in range(NT):
                    for n in range(4):
                        if t == 0:
                            pe.wait_ge(out_w[n], 16)
                        for k in range(NK):
                            last = nc.tensor.matmul(ps[:, 2 * t + n // 2, (n % 2) * 256:(n % 2 + 1) * 256], mixT[:, k, t * P:(t + 1) * P],
                                                    slot((5, 6, 7, 0)[n], NK)[:, k, :], start=k == 0, stop=k == NK - 1)
                    last.then_inc(h_ps, 1)
                for t in range(NT):
                    pe.wait_ge(h_v, 3 + t)
                    for c in range(NK):
                        last = nc.tensor.transpose(ps[:, 2 * t + c // 4, (c % 4) * P:(c % 4 + 1) * P], f_n[:, t, c * P:(c + 1) * P], ident[:])
                    last.then_inc(fT_ps, 1)
                pe.wait_ge(gf_in, 32)
                pe.wait_ge(fT_ok, NT)
                for t in range(NT):
                    for k in range(NK):
                        last = nc.tensor.matmul(ps[:, 0, t * NE:(t + 1) * NE], f_T[:, k, t * P:(t + 1) * P], wr_w[:, k, :],
                                                start=k == 0, stop=k == NK - 1)
                last.then_inc(lg_ps, 1)
                pe.wait_ge(b_in, 16)
                for a in range(4):
                    last = nc.tensor.transpose(ps[:, 1, a * P:(a + 1) * P], b1_rows[:, a, :], ident[:])
                last.then_inc(b1_ps, 1)

            @block.scalar
            def _(act):
                def gates(i):
                    for m in range(2):
                        for n in range(2):
                            act.wait_ge(mx_ps, i * 8 + 4 * m + n + 1)
                            if not is_first(i):
                                act.wait_ge(mx_ok, i * 2 - 1 + m)
                            nc.scalar.activation(gates_w[m][n], ps[:, 4 * m + n, :], ACT.Sigmoid).then_inc(mx_sg, 1)
                gates(0)
                with act.Fori(1, 4) as i:
                    gates(i)
                for t in range(NT):
                    act.wait_ge(h_ok, t + 1)
                    if t:
                        act.wait_ge(h_sq, t)
                    nc.scalar.activation(f_T[:, 0:2, :].rearrange("p a b -> p (a b)"), h3[:, t, :], ACT.Square,
                                         accum_out=stat[:, t:t + 1]).then_inc(h_sq, 1)
                act.wait_ge(h_v, 1)
                nc.scalar.activation(stat[:, 8:12], stat[:, 4:8], ACT.Sqrt).then_inc(h_sq, 1)
                for t in range(NT):
                    act.wait_ge(fT_ps, t + 1)
                    nc.scalar.activation(f_T[:, :, t * P:(t + 1) * P],
                                         ps[:, 2 * t:2 * t + 2, :].rearrange("p a (c n) -> p (a c) n", n=P), ACT.Copy).then_inc(fT_ok, 1)

            @block.vector
            def _(v):
                def products(i):
                    for m in range(2):
                        for n in range(2):
                            v.wait_ge(mx_ps, i * 8 + 4 * m + 3 + n)
                            v.wait_ge(mx_sg, i * 4 + 2 * m + n + 1)
                            nc.vector.tensor_tensor(gates_w[m][n], gates_w[m][n], ps[:, 4 * m + 2 + n, :], ALU.mult).then_inc(mx_pr, 1)
                        v.wait_ge(mx_pr, i * 4 + 2 * m + 2)
                        dst = mixT_f[:, bass.ds(i * 2 * SEQ + m * SEQ, SEQ)]
                        nc.vector.tensor_tensor(dst, gates_w[m][0], gates_w[m][1], ALU.add).then_inc(mx_ok, 1)
                products(0)
                with v.Fori(1, 4) as i:
                    products(i)
                v.wait_ge(x_in, 32 * NT)
                for t in range(NT):
                    v.wait_ge(h_ps, t + 1)
                    nc.vector.tensor_tensor(h3[:, t, :].rearrange("p (a b) -> p a b", a=2), h3[:, t, :].rearrange("p (a b) -> p a b", a=2),
                                            ps[:, 2 * t:2 * t + 2, :], ALU.add).then_inc(h_ok, 1)
                v.wait_ge(h_sq, NT)
                nc.vector.tensor_scalar(stat[:, 4:8], stat[:, 0:4], 1.0 / D, EPS, ALU.mult, ALU.add).then_inc(h_v, 1)
                v.wait_ge(h_sq, NT + 1)
                nc.vector.reciprocal(stat[:, 12:16], stat[:, 8:12]).then_inc(h_v, 1)
                v.wait_ge(h_v, 2)
                v.wait_ge(gf_in, 32)
                for t in range(NT):
                    nc.vector.scalar_tensor_tensor(f_n[:, t, :], h3[:, t, :], stat[:, 12 + t:13 + t], gf_bc, ALU.mult, ALU.mult).then_inc(h_v, 1)
                v.wait_ge(lg_ps, 1)
                nc.vector.tensor_tensor(lg, ps[:, 0, 0:NT * NE].rearrange("p (t e) -> p t e", t=NT),
                                        br_bc.unsqueeze(1).broadcast_to([P, NT, NE]), ALU.add).then_inc(b1_ok, 1)
                v.wait_ge(b1_ps, 1)
                nc.vector.tensor_copy(b1T[:, :], ps[:, 1, :]).then_inc(b1_ok, 1)

        top_ok = sem("top_ok")
        rt_v = sem("rt_v")
        rt_a = sem("rt_a")
        rt_p = sem("rt_p")
        rt_ps = sem("rt_ps")

        take_anew()
        top_v = take(NT * 8).rearrange("p (t k) -> p t k", t=NT)
        top_i = take(NT * 8).bitcast(U32).rearrange("p (t k) -> p t k", t=NT)
        top_f = take(NT * 8).rearrange("p (t k) -> p t k", t=NT)
        gate = take(NT * TOPK).rearrange("p (t k) -> p t k", t=NT)
        gsum = take(NT)
        one_hot = [take(NT * NE).rearrange("p (t e) -> p t e", t=NT) for _ in range(TOPK)]
        chosen = take(NT * NE).rearrange("p (t e) -> p t e", t=NT)
        rank = take(NT * NE).rearrange("p (t e) -> p t e", t=NT)
        rank_m = take(NT * NE)
        tmp_r = take(NT * NE).rearrange("p (t e) -> p t e", t=NT)
        place_m = take(NT * NE)
        g_dense = take(NT * NE).rearrange("p (t e) -> p t e", t=NT)
        g_T = take(SEQ)
        b2_w = take(D)
        iota_e = take(NE)
        iota_r = take(SLOTS + CAP)
        tok_id, tok_far = take(NT), take(NT)
        iota_i = take(SLOTS + CAP).bitcast(I32)
        most = take(8)
        trips_f = take(1)
        trips = take(2).bitcast(I32)
        after_route = used["main"]

        with nc.Block() as block:
            @block.sync
            def _(sp):
                sp.dma_start(b2_w[0:NE, :], b2).then_inc(b_in, 16)

            @block.gpsimd
            def _(pool):
                nc.gpsimd.iota(iota_i, pattern=[[1, SLOTS + CAP]], base=0, channel_multiplier=0).then_inc(rt_p, 1)
                pool.wait_ge(rt_p, 1)
                nc.gpsimd.tensor_copy(iota_r, iota_i).then_inc(rt_p, 1)
                nc.gpsimd.tensor_copy(iota_e, iota_i[:, 0:NE]).then_inc(rt_p, 1)
                pool.wait_ge(rt_p, 3)
                nc.gpsimd.iota(iota_i[:, 0:NT], pattern=[[P, NT]], base=0, channel_multiplier=1).then_inc(rt_p, 1)
                pool.wait_ge(rt_p, 4)
                nc.gpsimd.tensor_copy(tok_id, iota_i[:, 0:NT]).then_inc(rt_p, 1)

            @block.scalar
            def _(act):
                act.wait_ge(rt_v, 2)
                nc.scalar.activation(gate, gate, ACT.Exp).then_inc(rt_a, 1)

            @block.vector
            def _(v):
                step = [0]

                def then(ins):
                    step[0] += 1
                    ins.then_inc(rt_v, 1)
                    v.wait_ge(rt_v, step[0])
                for t in range(NT):
                    nc.vector.max(top_v[:, t, :], lg[:, t, :]).then_inc(top_ok, 1)
                v.wait_ge(top_ok, NT)
                for t in range(NT):
                    nc.vector.max_index(top_i[:, t, :], top_v[:, t, :], lg[:, t, :]).then_inc(top_ok, 1)
                v.wait_ge(top_ok, 2 * NT)
                then(nc.vector.tensor_copy(top_f, top_i))
                then(nc.vector.tensor_tensor(gate, top_v[:, :, 0:TOPK], top_v[:, :, 0:1].broadcast_to([P, NT, TOPK]), ALU.subtract))
                v.wait_ge(rt_a, 1)
                then(nc.vector.tensor_reduce(gsum, gate, AX.X, ALU.add))
                then(nc.vector.reciprocal(gsum, gsum))
                then(nc.vector.tensor_tensor(gate, gate, gsum.unsqueeze(2).broadcast_to([P, NT, TOPK]), ALU.mult))
                v.wait_ge(rt_p, 5)
                for k in range(TOPK):
                    then(nc.vector.tensor_tensor(one_hot[k], iota_e.unsqueeze(1).broadcast_to([P, NT, NE]),
                                                 top_f[:, :, k:k + 1].broadcast_to([P, NT, NE]), ALU.is_equal))
                then(nc.vector.tensor_tensor(chosen, one_hot[0], one_hot[1], ALU.add))
                then(nc.vector.tensor_tensor(chosen, chosen, one_hot[2], ALU.add))
                then(nc.vector.tensor_tensor(chosen, chosen, one_hot[3], ALU.add))
                for k in range(TOPK):
                    dst = g_dense if k == 0 else tmp_r
                    then(nc.vector.tensor_tensor(dst, one_hot[k], gate[:, :, k:k + 1].broadcast_to([P, NT, NE]), ALU.mult))
                    if k:
                        then(nc.vector.tensor_tensor(g_dense, g_dense, tmp_r, ALU.add))
                v.wait_ge(rt_ps, 1)
                then(nc.vector.tensor_copy(rank, ps[:, 2, 0:NT * NE].rearrange("p (t e) -> p t e", t=NT)))
                then(nc.vector.tensor_reduce(most[:, 0:1], ps[:, 3, 0:NE], AX.X, ALU.max))
                then(nc.vector.tensor_scalar(tmp_r, chosen, -FAR, FAR, ALU.mult, ALU.add))
                then(nc.vector.tensor_tensor(rank_m.rearrange("p (e t) -> p t e", t=NT), tmp_r, rank, ALU.add))
                then(nc.vector.tensor_scalar(tok_far, tok_id, -FAR, None, ALU.add))
                then(nc.vector.tensor_copy(tmp_r, tok_far.unsqueeze(2).broadcast_to([P, NT, NE])))
                for k in range(1, TOPK):
                    then(nc.vector.scalar_tensor_tensor(tmp_r, one_hot[k], float(k * SEQ), tmp_r, ALU.mult, ALU.add))
                then(nc.vector.tensor_copy(place_m.rearrange("p (e t) -> p t e", t=NT), tmp_r))
                then(nc.vector.memset(trips_f, float(NE - 1)))
                for r in range(1, ROUNDS):
                    then(nc.vector.tensor_scalar(most[:, 1:2], most[:, 0:1], float(r * CAP), float(NE), ALU.is_gt, ALU.mult))
                    then(nc.vector.tensor_tensor(trips_f, trips_f, most[:, 1:2], ALU.add))
                then(nc.vector.tensor_copy(trips[:, 0:1], trips_f))
                then(nc.vector.tensor_scalar(trips_f, trips_f, -1.0, None, ALU.add))
                then(nc.vector.tensor_copy(trips[:, 1:2], trips_f))
                v.wait_ge(rt_ps, 2)
                then(nc.vector.tensor_copy(g_T[0:NE, :], ps[0:NE, 4, :]))
                for t in range(NT):
                    v.wait_ge(rt_ps, 3 + t)
                    a = 2 * (t % 2)
                    ht = h3[:, t, :].rearrange("p (a b) -> p a b", a=2)
                    nc.vector.tensor_tensor(ht, ht, ps[:, a:a + 2, :], ALU.add).then_inc(h_ok, 1)

            @block.tensor
            def _(pe):
                pe.wait_ge(rt_v, 12)
                for t in range(NT):
                    for u in range(t + 1):
                        last = nc.tensor.matmul(ps[:, 2, t * NE:(t + 1) * NE], (ones if u < t else below)[:], chosen[:, u, :],
                                                start=u == 0, stop=u == t)
                for t in range(NT):
                    last = nc.tensor.matmul(ps[:, 3, 0:NE], ones[:], chosen[:, t, :], start=t == 0, stop=t == NT - 1)
                last.then_inc(rt_ps, 1)
                pe.wait_ge(rt_v, 19)
                for t in range(NT):
                    last = nc.tensor.transpose(ps[0:NE, 4, t * P:(t + 1) * P], g_dense[:, t, :], ident[:])
                last.then_inc(rt_ps, 1)
                pe.wait_ge(b_in, 32)
                pe.wait_ge(rt_v, 44)
                for t in range(NT):
                    if t >= 2:
                        pe.wait_ge(h_ok, NT + t - 1)
                    for n in range(2):
                        last = nc.tensor.matmul(ps[:, 2 * (t % 2) + n, :], g_T[0:NE, t * P:(t + 1) * P], b2_w[0:NE, n * 512:(n + 1) * 512],
                                                start=True, stop=True)
                    last.then_inc(rt_ps, 1)

        s_oh = sem("s_oh")
        ix_ps = sem("ix_ps")
        ix_ok = sem("ix_ok")
        to_ok = sem("to_ok")
        xe_in = sem("xe_in")
        xeT_ps = sem("xeT_ps")
        xeT_ok = sem("xeT_ok")
        l1_used = sem("l1_used")
        b1_add = sem("b1_add")
        clamp = sem("clamp")
        sig_ok = sem("sig_ok")
        glu = sem("glu")
        act_ok = sem("act_ok")
        a_hi_ok = sem("a_hi_ok")
        a_lo_ok = sem("a_lo_ok")
        w_hi_ok = sem("w_hi_ok")
        w_lo_ok = sem("w_lo_ok")
        l2_used = sem("l2_used")
        ye_ok = sem("ye_ok")
        ye_out = sem("ye_out")

        take_anew(after_route)
        sel = take(NT * CAP).rearrange("p (t s) -> p t s", t=NT)
        ix_i, to_i = take(1).bitcast(I32), take(1).bitcast(I32)
        to_f = take(4)
        xe = take(D)
        xeT_f = take(NK * CAP)
        xeT = xeT_f.rearrange("p (c s) -> p c s", c=NK)
        g_w, l_w, sg_w, a_w = (take(NK * CAP) for _ in range(4))
        ye = take(D)
        assert used["main"] <= TEMPS - NT * D
        before_experts.close()
        a_hi, a_lo = (ctx.enter_context(nc.sbuf_tensor(n, [P, NK * CAP], F32R)) for n in ("act_high", "act_low"))
        aT_hi, aT_lo = (a[:, :].rearrange("p (c s) -> p c s", c=NK) for a in (a_hi, a_lo))
        w_hi, w_lo = (ctx.enter_context(nc.sbuf_tensor(n, [P, 4 * D], F32R)) for n in ("w2_high", "w2_low"))

        def slots_dve(v, it):
            e, r = it % NE, it // NE
            if not is_first(it):
                v.wait_ge(ix_ps, it)
            nc.vector.tensor_tensor(sel, iota_r[:, bass.ds(r * CAP, CAP)].unsqueeze(1).broadcast_to([P, NT, CAP]),
                                    rank_m[:, bass.ds(e * NT, NT)].unsqueeze(2).broadcast_to([P, NT, CAP]), ALU.is_equal).then_inc(s_oh, 1)

        def tokens_dve(v, it):
            v.wait_ge(ix_ps, it + 1)
            if not is_first(it):
                v.wait_ge(xe_in, it * 16)
            nc.vector.tensor_copy(ix_i[0:CAP, :], ps[0:CAP, 6, 400:401]).then_inc(ix_ok, 1)
            nc.vector.tensor_scalar(to_f[0:CAP, bass.ds(it % 4, 1)], ps[0:CAP, 6, 401:402], FAR, None, ALU.add).then_inc(ix_ok, 1)

        def slots_pe(pe, it):
            pe.wait_ge(s_oh, it + 1)
            if not is_first(it):
                pe.wait_ge(xeT_ok, it * 2)
            for t in range(NT):
                last = nc.tensor.matmul(ps[0:CAP, 6, 400:401], sel[:, t, :], tok_id[:, t:t + 1], start=t == 0, stop=t == NT - 1)
            for t in range(NT):
                last = nc.tensor.matmul(ps[0:CAP, 6, 401:402], sel[:, t, :], place_m[:, bass.ds((it % NE) * NT + t, 1)], start=t == 0, stop=t == NT - 1)
            last.then_inc(ix_ps, 1)

        def gather_pool(pool, it):
            pool.wait_ge(ix_ok, it * 2 + 1)
            if not is_first(it):
                pool.wait_ge(xeT_ps, it)
            alone(pool)
            pool.indirect_dma_start(out=xe[0:CAP, :], out_offset=None, in_=xn_d,
                                    in_offset=bass.IndirectOffsetOnAxis(ap=ix_i[0:CAP, :], axis=0)).then_inc(xe_in, 16)

        def places_dve(v, it):
            if not is_first(it):
                v.wait_ge(ye_out, it * 16)
            v.wait_ge(ix_ok, it * 2 + 2)
            nc.vector.tensor_copy(to_i[0:CAP, :], to_f[0:CAP, bass.ds(it % 4, 1)]).then_inc(to_ok, 1)

        def scatter_pool(pool, it):
            pool.wait_ge(ye_ok, it + 1)
            pool.wait_ge(to_ok, it + 1)
            alone(pool)
            pool.indirect_dma_start(out=res_d, out_offset=bass.IndirectOffsetOnAxis(ap=to_i[0:CAP, :], axis=0), in_=ye[0:CAP, :],
                                    in_offset=None, bounds_check=TOPK * SEQ - 1, oob_is_err=False).then_inc(ye_out, 16)

        def rows_pe(pe, it):
            pe.wait_ge(xe_in, it * 16 + 16)
            pe.wait_ge(ix_ok, it * 2 + 2)
            for c in range(NK):
                last = nc.tensor.transpose(ps[:, 6 + c // 4, (c % 4) * CAP:(c % 4 + 1) * CAP], xe[0:CAP, c * P:(c + 1) * P], ident[0:CAP, 0:CAP])
            last.then_inc(xeT_ps, 1)

        def rows_act(act, it):
            act.wait_ge(xeT_ps, it + 1)
            if not is_first(it):
                act.wait_ge(l1_used, it * 8)
            for b in range(2):
                nc.scalar.activation(xeT_f[:, b * 4 * CAP:(b + 1) * 4 * CAP], ps[:, 6 + b, 0:4 * CAP], ACT.Copy).then_inc(xeT_ok, 1)

        def up_pe(pe, it):
            pe.wait_ge(xeT_ok, it * 2 + 2)
            if not is_first(it):
                pe.wait_ge(b1_add, it * 2)
            for k in range(NK):
                pe.wait_ge(exp_w[k], it * 16 + 16)
                for m in range(2 * DFF // P):
                    last = nc.tensor.matmul(ps[:, m // 4, (m % 4) * CAP:(m % 4 + 1) * CAP], slot(k, 1)[:, 0, m * P:(m + 1) * P], xeT[:, k, :],
                                            start=k == 0 and m % 4 == 0, stop=k == NK - 1, skip_group_check=True)
                last.then_inc(l1_used, 1)

        def bias_dve(v, it):
            e = it % NE
            v.wait_ge(l1_used, it * 8 + 8)
            for i, dst in enumerate((g_w, l_w)):
                if not is_first(it):
                    v.wait_ge(act_ok, it)
                bias = b1T[:, bass.ds(e * 16 + 8 * i, 8)].rearrange("p (a c) -> p a c", a=2).unsqueeze(3).broadcast_to([P, 2, 4, CAP])
                nc.vector.tensor_tensor(dst.rearrange("p (a c s) -> p a c s", a=2, c=4),
                                        ps[:, 2 * i:2 * i + 2, 0:4 * CAP].rearrange("p a (c s) -> p a c s", c=4), bias, ALU.add).then_inc(b1_add, 1)

        def act_dve(v, it):
            v.wait_ge(b1_add, it * 2 + 1)
            nc.vector.tensor_scalar(g_w, g_w, LIMIT, None, ALU.min).then_inc(clamp, 1)
            v.wait_ge(b1_add, it * 2 + 2)
            nc.vector.tensor_scalar(l_w, l_w, LIMIT, -LIMIT, ALU.min, ALU.max).then_inc(clamp, 1)
            v.wait_ge(clamp, it * 2 + 2)
            nc.vector.scalar_tensor_tensor(l_w, l_w, 1.0, g_w, ALU.add, ALU.mult).then_inc(glu, 1)
            v.wait_ge(glu, it + 1)
            v.wait_ge(sig_ok, it + 1)
            if not is_first(it):
                v.wait_ge(a_lo_ok, it)
            nc.vector.tensor_tensor(a_w, l_w, sg_w, ALU.mult).then_inc(act_ok, 1)

        def act_act(act, it):
            act.wait_ge(clamp, it * 2 + 1)
            if not is_first(it):
                act.wait_ge(act_ok, it)
            nc.scalar.activation(sg_w, g_w, ACT.Sigmoid, scale=ALPHA).then_inc(sig_ok, 1)

        def split_act(act, it):
            act.wait_ge(act_ok, it + 1)
            if not is_first(it):
                act.wait_ge(l2_used, it * 8)
            nc.scalar.activation(a_hi[:, :], a_w, ACT.Copy).then_inc(a_hi_ok, 1)

        def split_dve(v, it):
            v.wait_ge(a_hi_ok, it + 1)
            nc.vector.tensor_tensor(a_lo[:, :], a_w, a_hi[:, :].bitcast(F32), ALU.subtract).then_inc(a_lo_ok, 1)

        def w2_rows(k):
            return slot(8 + k // 2, 2)[:, k % 2, :], slice((k % 4) * D, (k % 4 + 1) * D)

        def w2_act(act, it, ks, read):
            for k in ks:
                src, cols = w2_rows(k)
                if k % 2 == 0:
                    act.wait_ge(exp_w[8 + k // 2], it * 16 + 16)
                if k >= 4 or not is_first(it):
                    act.wait_ge(l2_used, read + k - 3)
                nc.scalar.activation(w_hi[:, cols], src, ACT.Copy).then_inc(w_hi_ok, 1)

        def w2_dve(v, it, ks):
            for k in ks:
                src, cols = w2_rows(k)
                v.wait_ge(w_hi_ok, it * 8 + k + 1)
                nc.vector.tensor_tensor(w_lo[:, cols], src, w_hi[:, cols].bitcast(F32), ALU.subtract).then_inc(w_lo_ok, 1)

        def down_pe(pe, it):
            pe.wait_ge(a_lo_ok, it + 1)
            if not is_first(it):
                pe.wait_ge(ye_ok, it)
            for k in range(NK):
                pe.wait_ge(w_lo_ok, it * 8 + k + 1)
                for n in range(2):
                    cols = slice((k % 4) * D + n * 512, (k % 4) * D + (n + 1) * 512)
                    for i, (a, w) in enumerate(((aT_hi, w_hi), (aT_hi, w_lo), (aT_lo, w_hi))):
                        last = nc.tensor.matmul(ps[0:CAP, 4 + n, :], a[:, k, :], w[:, cols],
                                                start=k == 0 and i == 0, stop=k == NK - 1 and i == 2)
                last.then_inc(l2_used, 1)

        def down_act(act, it):
            act.wait_ge(l2_used, it * 8 + 8)
            if not is_first(it):
                act.wait_ge(ye_out, it * 16)
            nc.scalar.activation(ye[0:CAP, :].rearrange("p (a b) -> p a b", a=2), ps[0:CAP, 4:6, :], ACT.Copy).then_inc(ye_ok, 1)

        def load_w1(sp, it):
            for u in range(NK):
                sp.wait_ge(l1_used, it * 8 + u - 7)
                load_expert(sp, it, u)

        def load_w2(sp, it):
            for u in range(8, 12):
                sp.wait_ge(w_lo_ok, it * 8 + 2 * u - 22)
                load_expert(sp, it, u)

        def load_w2_last(sp, before):
            for u in range(8, 12):
                sp.wait_ge(w_lo_ok, before * 8 + 2 * u - 14)
                load_expert(sp, before + 1, u)

        def pass_act(act, it):
            split_act(act, it - 1)
            w2_act(act, it - 1, range(4), (it - 1) * 8)
            rows_act(act, it + 1)
            w2_act(act, it - 1, range(4, 8), (it - 1) * 8)
            down_act(act, it - 1)
            act_act(act, it)

        def pass_dve(v, it):
            tokens_dve(v, it + 1)
            slots_dve(v, it + 2)
            split_dve(v, it - 1)
            w2_dve(v, it - 1, range(4))
            places_dve(v, it - 1)
            bias_dve(v, it)
            w2_dve(v, it - 1, range(4, 8))
            act_dve(v, it)

        def pass_before(eng):
            return eng.value_load(trips[0:1, 1:2], min_val=NE - 2, max_val=NE * ROUNDS - 2)

        def last_pass(eng):
            return eng.value_load(trips[0:1, 0:1], min_val=NE - 1, max_val=NE * ROUNDS - 1)

        with nc.Block() as block:
            @block.sync
            def _(sp):
                last, before = last_pass(sp), pass_before(sp)
                load_w1(sp, 1)
                with sp.Fori(2, last + 1, 2) as pair:
                    for it in (pair, pair + 1):
                        load_w1(sp, it)
                        load_w2(sp, it - 1)
                load_w2_last(sp, before)

            @block.gpsimd
            def _(pool):
                last = last_pass(pool)
                gather_pool(pool, 0)
                gather_pool(pool, 1)
                gather_pool(pool, 2)
                scatter_pool(pool, 0)
                with pool.Fori(2, last + 1, 2) as pair:
                    for it in (pair, pair + 1):
                        gather_pool(pool, it + 1)
                        scatter_pool(pool, it - 1)
                scatter_pool(pool, last)
                pool.wait_ge(xe_in, last * 16 + 32)
                pool.wait_ge(ye_out, last * 16 + 16)

            @block.tensor
            def _(pe):
                last = last_pass(pe)
                slots_pe(pe, 0)
                rows_pe(pe, 0)
                slots_pe(pe, 1)
                up_pe(pe, 0)
                rows_pe(pe, 1)
                slots_pe(pe, 2)
                up_pe(pe, 1)
                rows_pe(pe, 2)
                down_pe(pe, 0)
                with pe.Fori(2, last + 1, 2) as pair:
                    for it in (pair, pair + 1):
                        slots_pe(pe, it + 1)
                        up_pe(pe, it)
                        rows_pe(pe, it + 1)
                        down_pe(pe, it - 1)
                down_pe(pe, last)

            @block.scalar
            def _(act):
                last, before = last_pass(act), pass_before(act)
                rows_act(act, 0)
                rows_act(act, 1)
                act_act(act, 0)
                pass_act(act, 1)
                with act.Fori(2, last + 1, 2) as pair:
                    for it in (pair, pair + 1):
                        pass_act(act, it)
                split_act(act, last)
                w2_act(act, last, range(8), before * 8 + 8)
                down_act(act, last)

            @block.vector
            def _(v):
                last = last_pass(v)
                slots_dve(v, 0)
                tokens_dve(v, 0)
                slots_dve(v, 1)
                tokens_dve(v, 1)
                slots_dve(v, 2)
                bias_dve(v, 0)
                act_dve(v, 0)
                pass_dve(v, 1)
                with v.Fori(2, last + 1, 2) as pair:
                    for it in (pair, pair + 1):
                        pass_dve(v, it)
                places_dve(v, last)
                split_dve(v, last)
                w2_dve(v, last, range(8))

        r_in = out_w
        nf_bc, fin_junk = (weights[:, a * D:(a + 1) * D] for a in (NT * TOPK, NT * TOPK + 1))
        acc_ok = sem("acc_ok")
        rows4 = weights[:, 0:NT * TOPK * D].rearrange("p (t k d) -> p t k d", t=NT, k=TOPK)
        with nc.Block() as block:
            @block.vector
            def _(v):
                for t in range(NT):
                    v.wait_ge(r_in[t], 16 + 16 * TOPK)
                    for k in range(TOPK):
                        if k:
                            v.wait_ge(acc_ok, t * TOPK + k)
                        nc.vector.scalar_tensor_tensor(h3[:, t, :], rows4[:, t, k, :], gate[:, t, k:k + 1], h3[:, t, :],
                                                       ALU.mult, ALU.add).then_inc(acc_ok, 1)
                v.wait_ge(h_sq, 2 * NT + 1)
                nc.vector.tensor_scalar(stat[:, 4:8], stat[:, 0:4], 1.0 / D, EPS, ALU.mult, ALU.add).then_inc(h_v, 1)
                v.wait_ge(h_sq, 2 * NT + 2)
                nc.vector.reciprocal(stat[:, 12:16], stat[:, 8:12]).then_inc(h_v, 1)
                v.wait_ge(h_v, NT + 4)
                v.wait_ge(gf_in, 48)
                for t in range(NT):
                    nc.vector.scalar_tensor_tensor(h3[:, t, :], h3[:, t, :], stat[:, 12 + t:13 + t], nf_bc, ALU.mult, ALU.mult).then_inc(h_v, 1)

            @block.scalar
            def _(act):
                for t in range(NT):
                    act.wait_ge(acc_ok, (t + 1) * TOPK)
                    if t:
                        act.wait_ge(h_sq, NT + 1 + t)
                    nc.scalar.activation(fin_junk, h3[:, t, :], ACT.Square, accum_out=stat[:, t:t + 1]).then_inc(h_sq, 1)
                act.wait_ge(h_v, NT + 3)
                nc.scalar.activation(stat[:, 8:12], stat[:, 4:8], ACT.Sqrt).then_inc(h_sq, 1)

            @block.sync
            def _(sp):
                for t in range(NT):
                    for k in range(TOPK):
                        sp.dma_start(rows4[:, t, k, :], res_d[k * SEQ + t * P:k * SEQ + (t + 1) * P, :]).then_inc(r_in[t], 16)
                sp.dma_start(nf_bc, norm_final_g.rearrange("(a n) -> a n", a=1).broadcast_to([P, D])).then_inc(gf_in, 16)
                for t in range(NT):
                    sp.wait_ge(h_v, NT + 5 + t)
                    sp.dma_start(out[t * P:(t + 1) * P, :], h3[:, t, :]).then_inc(f_out, 16)
                sp.wait_ge(f_out, 32 * NT)

    return nc


_NAMES = ['x', 'norm_mix_g', 'w_in', 'gla_fw2_f', 'gla_fb_f', 'gla_fw2_b', 'gla_fb_b', 'gla_norm_g', 'conv_w', 'conv_b',
          'dt_bias_f', 'dt_bias_b', 'a_log_f', 'a_log_b', 'ssd_d', 'ssd_norm_g', 'w_up_gla', 'w_up_ssd', 'w_out',
          'norm_ffn_g', 'w_router', 'b_router', 'w1', 'b1', 'w2', 'b2', 'norm_final_g']


def kernel(**inputs):
    import concourse.bacc as bacc
    from concourse.bass_utils import run_bass_kernel_spmd

    nc = bacc.Bacc("TRN2", target_bir_lowering=False, num_devices=1)
    arrays, args = {}, []
    for name in _NAMES:
        a = np.ascontiguousarray(inputs[name])
        if name != 'norm_final_g':
            a = a[0]
        arrays[f"in_{name}"] = a
        args.append(nc.dram_tensor(f"in_{name}", a.shape, mybir.dt.from_np(a.dtype), kind="ExternalInput").ap())
    out = nc.dram_tensor("out", (SEQ, D), F32, kind="ExternalOutput").ap()
    build(nc, *args, out)
    r = run_bass_kernel_spmd(nc, [arrays], core_ids=[0])
    return r.results[0]["out"].reshape(1, SEQ, D)
```
